# Optimizing a Trainium2 kernel written in Bass

```python
import jax
import jax.numpy as jnp
from jax import lax

D_MODEL = 1024
BATCH = 1
SEQ = 1024
DEPTH = 1

CHUNK = 64
QBLOCK = 128
EPS = 1e-6

GLA_HEADS = 4
GLA_DK = 64
GLA_DV = 128
GLA_GATE_RANK = 16
GLA_GATE_NORMALIZER = 16.0
GLA_LOG_GATE_MIN = -1.0

MLA_HEADS = 8
MLA_Q_RANK = 256
MLA_KV_RANK = 128
MLA_NOPE = 64
MLA_ROPE = 32
MLA_V = 64
ROPE_BASE = 10000.0

GLA_QK_W = GLA_HEADS * GLA_DK
GLA_V_W = GLA_HEADS * GLA_DV
D_PROJ = 2 * GLA_QK_W + 2 * GLA_V_W + GLA_GATE_RANK + MLA_Q_RANK + MLA_KV_RANK + MLA_ROPE
D_MIX = GLA_V_W + MLA_HEADS * MLA_V

D_FF = 4 * D_MODEL

kernel_name = 'hymba_gla_mla_sqrelu_chunk_causal'

def _rmsnorm(x, g):
    xf = x.astype(jnp.float32)
    y = xf * lax.rsqrt(jnp.mean(xf * xf, axis=-1, keepdims=True) + EPS)
    return (y * g.astype(jnp.float32)).astype(x.dtype)

def _proj_split_points():
    widths = (GLA_QK_W, GLA_QK_W, GLA_V_W, GLA_GATE_RANK, GLA_V_W, MLA_Q_RANK, MLA_KV_RANK)
    pts, acc = [], 0
    for w in widths:
        acc += w
        pts.append(acc)
    return pts

def _gla_chunked(q, k, v, log_a):
    b_, s_, h_, dk = q.shape
    dv = v.shape[-1]
    n = s_ // CHUNK

    def to_chunks(t):
        return t.astype(jnp.float32).reshape(b_, n, CHUNK, h_, t.shape[-1]).transpose(0, 3, 1, 2, 4)

    q, k, v, log_a = to_chunks(q), to_chunks(k), to_chunks(v), to_chunks(log_a)
    cum = jnp.cumsum(log_a, axis=3)
    q_dec = q * (dk ** -0.5) * jnp.exp(cum)
    k_inv = k * jnp.exp(-cum)
    causal = jnp.tril(jnp.ones((CHUNK, CHUNK), dtype=bool))
    scores = jnp.where(causal, jnp.einsum('bhncd,bhnjd->bhncj', q_dec, k_inv), 0.0)
    o_intra = jnp.einsum('bhncj,bhnjv->bhncv', scores, v)

    cum_last = cum[:, :, :, -1, :]
    k_to_end = k * jnp.exp(cum_last[:, :, :, None, :] - cum)
    chunk_kv = jnp.einsum('bhncd,bhncv->bhndv', k_to_end, v)

    def step(state, inp):
        decay, kv = inp
        return jnp.exp(decay)[..., None] * state + kv, state

    init = jnp.zeros((b_, h_, dk, dv), jnp.float32)
    _, prev = lax.scan(step, init, (jnp.moveaxis(cum_last, 2, 0), jnp.moveaxis(chunk_kv, 2, 0)))
    prev = jnp.moveaxis(prev, 0, 2)
    o = o_intra + jnp.einsum('bhncd,bhndv->bhncv', q_dec, prev)
    return o.transpose(0, 2, 3, 1, 4).reshape(b_, s_, h_, dv)

def _rope_tables(positions):
    inv_freq = ROPE_BASE ** (-jnp.arange(0, MLA_ROPE, 2, dtype=jnp.float32) / MLA_ROPE)
    ang = positions.astype(jnp.float32)[..., None] * inv_freq
    return jnp.cos(ang)[:, :, None, :], jnp.sin(ang)[:, :, None, :]

def _apply_rope(x, cos, sin):
    half = MLA_ROPE // 2
    xf = x.astype(jnp.float32)
    x1, x2 = xf[..., :half], xf[..., half:]
    return jnp.concatenate([x1 * cos - x2 * sin, x1 * sin + x2 * cos], axis=-1).astype(x.dtype)

def _chunk_causal_attention(q, k, v):
    b_, s_, h_, dqk = q.shape
    dv = v.shape[-1]
    nb = s_ // QBLOCK
    scale = dqk ** -0.5
    qb = q.reshape(b_, nb, QBLOCK, h_, dqk).transpose(1, 0, 3, 2, 4)
    kh = k.transpose(0, 2, 1, 3)
    vh = v.transpose(0, 2, 1, 3)
    key_chunk = jnp.arange(s_) // CHUNK

    def one_block(args):
        q_blk, blk = args
        s = jnp.einsum('bhqd,bhkd->bhqk', q_blk, kh, preferred_element_type=jnp.float32) * scale
        q_chunk = (blk * QBLOCK + jnp.arange(QBLOCK)) // CHUNK
        mask = key_chunk[None, :] <= q_chunk[:, None]
        p = jax.nn.softmax(jnp.where(mask, s, -1e30), axis=-1)
        return jnp.einsum('bhqk,bhkv->bhqv', p.astype(vh.dtype), vh)

    out = lax.map(one_block, (qb, jnp.arange(nb)))
    return out.transpose(1, 0, 3, 2, 4).reshape(b_, s_, h_ * dv)

def setup_inputs(seed: int = 0) -> dict:
    key = jax.random.key(seed)
    ks = jax.random.split(key, 20)
    f32 = jnp.float32

    def w(k, shape, fan_in):
        return jax.random.normal(k, shape, f32) * fan_in ** -0.5

    def gain(k, shape):
        return 1.0 + 0.05 * jax.random.normal(k, shape, f32)

    x = jax.random.normal(ks[0], (BATCH, SEQ, D_MODEL), f32)
    offset = jax.random.randint(ks[1], (BATCH, 1), 0, 64, dtype=jnp.int32) * CHUNK
    positions = (offset + jnp.arange(SEQ, dtype=jnp.int32)[None, :]).astype(jnp.int32)
    return {
        'x': x,
        'positions': positions,
        'attn_norm': gain(ks[2], (DEPTH, D_MODEL)),
        'w_in': w(ks[3], (DEPTH, D_MODEL, D_PROJ), D_MODEL),
        'w_gate_up': w(ks[4], (DEPTH, GLA_GATE_RANK, GLA_QK_W), GLA_GATE_RANK),
        'b_gate': 0.1 * jax.random.normal(ks[5], (DEPTH, GLA_QK_W), f32),
        'gla_out_norm': gain(ks[6], (DEPTH, GLA_DV)),
        'q_a_norm': gain(ks[7], (DEPTH, MLA_Q_RANK)),
        'w_uq': w(ks[8], (DEPTH, MLA_Q_RANK, MLA_HEADS * (MLA_NOPE + MLA_ROPE)), MLA_Q_RANK),
        'kv_a_norm': gain(ks[9], (DEPTH, MLA_KV_RANK)),
        'w_ukv': w(ks[10], (DEPTH, MLA_KV_RANK, MLA_HEADS * (MLA_NOPE + MLA_V)), MLA_KV_RANK),
        'q_head_norm': gain(ks[11], (DEPTH, MLA_NOPE + MLA_ROPE)),
        'k_head_norm': gain(ks[12], (DEPTH, MLA_NOPE + MLA_ROPE)),
        'w_out': w(ks[13], (DEPTH, D_MIX, D_MODEL), D_MIX),
        'mlp_norm': gain(ks[14], (DEPTH, D_MODEL)),
        'w_up': w(ks[15], (DEPTH, D_MODEL, D_FF), D_MODEL),
        'w_down': w(ks[16], (DEPTH, D_FF, D_MODEL), D_FF),
    }

def reference(x, positions, attn_norm, w_in, w_gate_up, b_gate, gla_out_norm, q_a_norm, w_uq,
              kv_a_norm, w_ukv, q_head_norm, k_head_norm, w_out, mlp_norm, w_up, w_down):
    b_, s_, _ = x.shape
    cos, sin = _rope_tables(positions)
    split_pts = _proj_split_points()
    for l in range(DEPTH):
        h = _rmsnorm(x, attn_norm[l])
        z = h @ w_in[l]
        zq, zk, zv, zgate, zg, zcq, zckv, zkpe = jnp.split(z, split_pts, axis=-1)

        gq = zq.reshape(b_, s_, GLA_HEADS, GLA_DK)
        gk = zk.reshape(b_, s_, GLA_HEADS, GLA_DK)
        gv = zv.reshape(b_, s_, GLA_HEADS, GLA_DV)
        gate_logit = (zgate @ w_gate_up[l] + b_gate[l]).astype(jnp.float32)
        log_a = jnp.maximum(jax.nn.log_sigmoid(gate_logit) / GLA_GATE_NORMALIZER, GLA_LOG_GATE_MIN)
        log_a = log_a.reshape(b_, s_, GLA_HEADS, GLA_DK)
        o_gla = _gla_chunked(gq, gk, gv, log_a).astype(x.dtype)
        o_gla = _rmsnorm(o_gla, gla_out_norm[l]) * jax.nn.silu(zg.reshape(b_, s_, GLA_HEADS, GLA_DV))
        o_gla = o_gla.reshape(b_, s_, GLA_V_W)

        q = (_rmsnorm(zcq, q_a_norm[l]) @ w_uq[l]).reshape(b_, s_, MLA_HEADS, MLA_NOPE + MLA_ROPE)
        kv = (_rmsnorm(zckv, kv_a_norm[l]) @ w_ukv[l]).reshape(b_, s_, MLA_HEADS, MLA_NOPE + MLA_V)
        k_nope, v = kv[..., :MLA_NOPE], kv[..., MLA_NOPE:]
        k_pe = jnp.broadcast_to(zkpe[:, :, None, :], (b_, s_, MLA_HEADS, MLA_ROPE))
        k = jnp.concatenate([k_nope, k_pe], axis=-1)
        q = _rmsnorm(q, q_head_norm[l])
        k = _rmsnorm(k, k_head_norm[l])
        q = jnp.concatenate([q[..., :MLA_NOPE], _apply_rope(q[..., MLA_NOPE:], cos, sin)], axis=-1)
        k = jnp.concatenate([k[..., :MLA_NOPE], _apply_rope(k[..., MLA_NOPE:], cos, sin)], axis=-1)
        o_mla = _chunk_causal_attention(q, k, v)

        x = x + jnp.concatenate([o_gla, o_mla], axis=-1) @ w_out[l]

        h = _rmsnorm(x, mlp_norm[l])
        x = x + jnp.square(jax.nn.relu(h @ w_up[l])) @ w_down[l]
    return x


_drawn_inputs = setup_inputs


def setup_inputs(seed=0):
    import zlib

    import numpy as np

    out = dict(_drawn_inputs(seed))
    spreads = {}
    factors = {'b_gate': 15.71,
     'q_a_norm': 8.0,
     'kv_a_norm': 7.91,
     'q_head_norm': 8.0,
     'k_head_norm': 8.0,
     'w_gate_up': 7.217,
     'gla_out_norm': 8.0,
     'mlp_norm': 4.596}
    for name, (base, spread) in spreads.items():
        noise = np.random.default_rng([zlib.crc32(name.encode()), seed]).standard_normal(out[name].shape)
        drawn = base * np.exp(spread * noise) if base else spread * noise
        out[name] = jnp.asarray(drawn.astype(out[name].dtype))
    for name, factor in factors.items():
        out[name] = (out[name] * factor).astype(out[name].dtype)
    return out
```

```python
from contextlib import ExitStack

import concourse.bass as bass
from concourse import mybir

F32 = mybir.dt.float32
F32R = mybir.dt.float32r
I32 = mybir.dt.int32
ALU = mybir.AluOpType
ACT = mybir.ActivationFunctionType
AX = mybir.AxisListType

P = 128
T, D, FF = 1024, 1024, 4096
NB = T // P
KT = D // P
W = 512
NH = D // W
EPS = 1e-6

CHUNK = 64
GH, GDK, GDV, GR = 4, 64, 128, 16
GT = GH * GDK // P
GATE_NORM, LOG_GATE_MIN = 16.0, -1.0

MH, QR, KVR, NOPE, ROPE, MV = 8, 256, 128, 64, 32, 64
DQK = NOPE + ROPE
HALF = ROPE // 2
ROPE_BASE = 10000.0
SCALE = float(DQK) ** -0.5
MASKED = -1e30

C_QK, C_V, C_GATE, C_G, C_MLA = 0, 512, 1024, 1040, 1552
MLA_W = QR + KVR + ROPE
ZM = MLA_W + GR

RING = 4
FG = FF // W
FT = W // P
IN_GROUPS, OUT_GROUPS = 4, NH

TWO_PI = 6.283185307179586
TWO_PI_A = 6.28125
TWO_PI_B = 0.0019350051879882812
TWO_PI_C = TWO_PI - TWO_PI_A - TWO_PI_B
ROUND = 12582912.0
PI_SAFE = 3.1415925


def layer(nc, x, positions, attn_norm, w_in, w_gate_up, b_gate, gla_out_norm, q_a_norm, w_uq,
          kv_a_norm, w_ukv, q_head_norm, k_head_norm, w_out, mlp_norm, w_up, w_down, out):
    x_d = x[0].rearrange("(b p) d -> b p d", p=P)
    out_d = out[0].rearrange("(b p) d -> b p d", p=P)
    w_in_d = w_in[0].rearrange("(k p) n -> k p n", p=P)
    w_out_d = w_out[0].rearrange("(k p) (h n) -> h k p n", p=P, n=W)
    w_up_d = w_up[0].rearrange("(k p) (g n) -> g k p n", p=P, n=W)
    w_down_d = w_down[0].rearrange("(g f p) (h n) -> g f h p n", p=P, f=FT, n=W)

    ctx = ExitStack()
    with ctx:
        ctx.enter_context(nc.allow_non_contiguous_dma(reason="gains and positions of a few KB, laid by partition"))

        def sem(name):
            return ctx.enter_context(nc.semaphore(name))

        base = -(-nc.sbuf_base // 64) * 64
        KB = 1024

        def at(name, shape, offset, dt=F32):
            return nc.alloc_sbuf_tensor_at(name, shape, dt, offset=base + offset)

        A, B, X, E, RAW, GB, C = 0, 64 * KB, 128 * KB, 160 * KB, 192 * KB, 200 * KB, 204 * KB
        a_hi = at("a_hi", [P, KT, T], A, F32R)
        a_lo = at("a_lo", [P, KT, T], A + 32 * KB, F32R)
        w_hi = at("w_hi", [P, 2, KT, W], B, F32R)
        w_lo = at("w_lo", [P, 2, KT, W], B + 32 * KB, F32R)
        xs = at("xs", [P, NB, D], X)
        zqk = xs[:, :, 0:W]
        zv = xs[:, :, W:2 * W]
        zm = at("zm", [P, NB, ZM], E)
        rk = at("rk", [P, NB, HALF], E)
        rt = at("rt", [P, NB, HALF], E + 512)
        freq = at("freq", [P, HALF], E + 1024)
        zg = at("zg", [P, NB, W], E + 14 * KB)
        act_hi = at("act_hi", [P, FT, T], E, F32R)
        act_lo = at("act_lo", [P, FT, T], E + 16 * KB, F32R)
        xn2 = at("xn2", [P, 2, D], E + 24 * KB)
        raw = at("raw", [P, RING, W], RAW)
        gain = at("gain", [P, D], GB)
        gqk = at("gqk", [P, 2, DQK], GB)
        gn = at("gn", [P, GDV], GB + 768)
        wgate = at("wgate", [GR, GH * GDK], GB + 1280)
        relu = at("relu", [P, 2, W], GB)

        gT = [at(f"gT{n}", [P, GT, T], B + 8 * KB * n) for n in range(8)]
        g_q, g_k, g_log, g_cum, g_qs, g_ks, g_ke, g_qf = gT
        zgateT = at("zgateT", [GR, T], B + 56 * KB)
        ones = at("ones", [P, P], B + 60 * KB)
        tanh_g = at("tanh_g", [P, NB, W], A + 16 * KB)
        sc = at("sc", [P, 2, GH, P], B)
        og = at("og", [P, 2, GH, GDV], B + 4 * KB)
        state = at("state", [P, 2, GT, 2 * GDV], B + 8 * KB)
        osq = at("osq", [P, 2, GH, GDV], B + 12 * KB)
        ke_tok = xs[:, :, 0:GH * GDK]

        m_kT = at("m_kT", [DQK, MH, T], B)
        m_v = at("m_v", [P, NB, MH * MV], B + 32 * KB)
        m_uq = at("m_uq", [P, QR // P, MH * DQK], B + 48 * KB)
        m_ukv = at("m_ukv", [P, MH * (NOPE + MV)], B + 54 * KB)
        m_cT = at("m_cT", [P, 2, 3, P], B + 58 * KB)
        m_qk = at("m_qk", [P, 2, 2 * MH, DQK], X)
        m_p = at("m_p", [P, 2, T], X + 12 * KB)
        m_pT = at("m_pT", [P, 2, NB, P], X + 20 * KB)
        m_qT = at("m_qT", [DQK, 2, MH, P], E + 14 * KB)
        m_sq = at("m_sq", [P, 2 * MH, DQK], E + 22 * KB)
        m_rc = at("m_rc", [P, 2 * MH, 2, HALF], E + 28 * KB)
        m_rs = at("m_rs", [P, 2 * MH, 2, HALF], E + 30 * KB)

        place = [C]

        def small(name, shape, dt=F32):
            size = 4
            for n in shape[1:]:
                size *= n
            t = at(name, shape, place[0], dt)
            place[0] += -(-size // 32) * 32
            return t

        ident = small("ident", [P, P])
        causal = small("causal", [P, P], I32)
        cos = small("cos", [P, NB, HALF])
        sin = small("sin", [P, NB, HALF])
        pos = small("pos", [P, NB], I32)
        minus_half = small("minus_half", [P, 2 * MH])
        bg = small("bg", [P, GT])
        ga = small("ga", [P, 3])
        ssq = small("ssq", [P, 2, NB])
        rstd = small("rstd", [P, 2, NB])
        decay = small("decay", [P, GT, NB])
        g_ss = small("g_ss", [P, 2, GH])
        g_rs = small("g_rs", [P, 2, GH])
        c_ss = small("c_ss", [P, 2, NB])
        c_rs = small("c_rs", [P, 2, NB])
        h_ss = small("h_ss", [P, 2 * MH])
        h_rs = small("h_rs", [P, 2 * MH])
        m_nm = small("m_nm", [P, 2])
        m_sum = small("m_sum", [P, 2])
        m_rden = small("m_rden", [P, 2])
        assert base + place[0] <= nc.sbuf_usable_end

        ps = ctx.enter_context(nc.psum_tensor("ps", [P, 8, W], F32))

        def bank4(n, parts=P):
            return ps[0:parts, n, :].rearrange("p (h c) -> p h c", c=P)

        x_in = [sem(f"x_in{b}") for b in range(NB)]
        raw_in = [sem(f"raw_in{s}") for s in range(RING)]
        gain_in, consts_in, phase_in, mla_w_in = sem("gain_in"), sem("consts_in"), sem("phase_in"), sem("mla_w_in")
        stored = sem("stored")
        ident_ready, pool_step, dve_step, act_step = sem("ident_ready"), sem("pool_step"), sem("dve_step"), sem("act_step")
        whi_done, wlo_done = sem("whi_done"), sem("wlo_done")
        ssq_ready, rstd_ready, xn_ready = sem("ssq_ready"), sem("rstd_ready"), sem("xn_ready")
        xT_ready, ahi_done, alo_done = sem("xT_ready"), sem("ahi_done"), sem("alo_done")
        z_ready, z_out = sem("z_ready"), sem("z_out")
        rope_arg, rope_ready = sem("rope_arg"), sem("rope_ready")
        qkT_ready, qkT_out, gateT_ready, gateT_out = sem("qkT_ready"), sem("qkT_out"), sem("gateT_ready"), sem("gateT_out")
        logit_ready, logit_out, softplus_ready = sem("logit_ready"), sem("logit_out"), sem("softplus_ready")
        from_mid, to_last, g_exp = sem("from_mid"), sem("to_last"), sem("g_exp")
        qs_ready, ke_ready, keT_ready, keT_out = sem("qs_ready"), sem("ke_ready"), sem("keT_ready"), sem("keT_out")
        tanh_ready, zg_ready = sem("tanh_ready"), sem("zg_ready")
        scT_ready, sc_ready, sc_zero, kv_ready, state_ready = sem("scT_ready"), sem("sc_ready"), sem("sc_zero"), sem("kv_ready"), sem("state_ready")
        o_ready, osq_ready, g_ss_ready, g_rs_ready, og_ready = sem("o_ready"), sem("osq_ready"), sem("g_ss_ready"), sem("g_rs_ready"), sem("og_ready")
        ogT_ready, g_mix_hi, g_mix_lo = sem("ogT_ready"), sem("g_mix_hi"), sem("g_mix_lo")
        qf_ready = sem("qf_ready")
        c_ss_ready, c_rs_ready, c_ready = sem("c_ss_ready"), sem("c_rs_ready"), sem("c_ready")
        job_ready, job_out = sem("job_ready"), sem("job_out")
        gqk_ready, sq_ready, h_ss_ready, qk_ready = sem("gqk_ready"), sem("sq_ready"), sem("h_ss_ready"), sem("qk_ready")
        s_ready, max_ready, p_ready, pn_ready = sem("s_ready"), sem("max_ready"), sem("p_ready"), sem("pn_ready")
        pT_ready, pT_out, pT_out2, pv_done = sem("pT_ready"), sem("pT_out"), sem("pT_out2"), sem("pv_done")
        m_mix_hi, m_mix_lo = sem("m_mix_hi"), sem("m_mix_lo")
        up_ready, up_bank_free, relu_ready = sem("up_ready"), sem("up_bank_free"), sem("relu_ready")
        acthi_done, actlo_done, y_ready, y_bank_free = sem("acthi_done"), sem("actlo_done"), sem("y_ready"), sem("y_bank_free")

        block = ctx.enter_context(nc.Block())

        def raw_value(q, k):
            n = 2 * q + k // RING + 1
            return 16 * n + (16 * (k // RING + 1) if isinstance(q, int) and q == 0 else 32)

        Q_UP = IN_GROUPS + OUT_GROUPS

        STEPS = [(b, h) for b in range(NB) for h in range(MH)]
        JOBS = {0: (0,), 1: (1, 2), 2: (3, 4), 5: (5, 6), 6: (7, 8)}
        NJOB = 9

        @block.sync
        def _(sp):
            def piece(q, k, src):
                if not (isinstance(q, int) and q == 0 and k < RING):
                    sp.wait_ge(wlo_done, KT * q + k - RING + 1)
                sp.dma_start(raw[:, k % RING, 0:src.shape[-1]], src).then_inc(raw_in[k % RING], 16)

            for k in range(KT):
                piece(0, k, w_in_d[k, :, C_MLA:C_MLA + MLA_W])
                sp.dma_start(raw[:, k % RING, MLA_W:ZM],
                             w_in_d[k, :, C_GATE:C_GATE + GR]).then_inc(raw_in[k % RING], 16)
            for q, c in ((1, C_QK), (2, C_V), (3, C_G)):
                for k in range(KT):
                    piece(q, k, w_in_d[k, :, c:c + W])
            for k in range(RING):
                piece(IN_GROUPS, k, w_out_d[0, k])
            sp.wait_ge(o_ready, NB)
            sp.dma_start(m_uq[:, :, :], w_uq[0].rearrange("(k p) n -> p k n", p=P)).then_inc(mla_w_in, 16)
            sp.dma_start(m_ukv[:, :], w_ukv[0]).then_inc(mla_w_in, 16)
            sp.wait_ge(pv_done, len(STEPS))
            sp.wait_ge(qk_ready, NB)
            for b in range(NB):
                sp.dma_start(xs[:, b, :], x_d[b]).then_inc(x_in[b], 16)
            for k in range(RING, KT):
                piece(IN_GROUPS, k, w_out_d[0, k])
            for n in range(1, NH):
                for k in range(KT):
                    piece(IN_GROUPS + n, k, w_out_d[n, k])

            def mlp_pieces(g):
                for k in range(KT):
                    piece(Q_UP + 2 * g, k, w_up_d[g, k])
                for k in range(KT):
                    piece(Q_UP + 1 + 2 * g, k, w_down_d[g, k // NH, k % NH])

            with sp.Fori(0, FG) as g:
                mlp_pieces(g)
            for b in range(NB):
                sp.wait_ge(y_bank_free, 4 + 2 * NB * (FG - 1) + 2 * b + 2)
                sp.dma_start(out_d[b], xs[:, b, :]).then_inc(stored, 16)
            sp.wait_ge(stored, 16 * NB)

        @block.gpsimd
        def _(pool):
            steps = [0]

            def step(ins):
                steps[0] += 1
                ins.then_inc(pool_step, 1)
                pool.wait_ge(pool_step, steps[0])

            def rsqrt(dst, src, n, ready):
                step(pool.tensor_scalar(dst, src, 1.0 / n, EPS, ALU.mult, ALU.add))
                pool.tensor_tensor(dst, dst, minus_half[:, 0:dst.shape[-1]], ALU.pow).then_inc(ready, 1)

            def low_part(q, k):
                s = k % RING
                pool.wait_ge(whi_done, KT * q + k + 1)
                width = ZM if isinstance(q, int) and q == 0 else W
                b = q % 2 if isinstance(q, int) else None
                dst = w_lo[:, b, k, 0:width]
                pool.tensor_tensor(dst, raw[:, s, 0:width], w_hi[:, b, k, 0:width].bitcast(F32),
                                   ALU.subtract).then_inc(wlo_done, 1)

            def low_part_at(half, count, k):
                pool.wait_ge(whi_done, count + k + 1)
                pool.tensor_tensor(w_lo[:, half, k, :], raw[:, k % RING, :],
                                   w_hi[:, half, k, :].bitcast(F32), ALU.subtract).then_inc(wlo_done, 1)

            pool.dma_start(gain[:, :], attn_norm[0].partition_broadcast(P)).then_inc(gain_in, 16)
            pool.dma_start(pos[:, :], positions[0].rearrange("(b p) -> p b", p=P)).then_inc(consts_in, 16)
            pool.dma_start(bg[:, :], b_gate[0].rearrange("(t p) -> p t", p=P)).then_inc(consts_in, 16)
            pool.dma_start(ga[:, 0:2], q_a_norm[0].rearrange("(t p) -> p t", p=P)).then_inc(consts_in, 16)
            pool.dma_start(ga[:, 2:3], kv_a_norm[0].rearrange("(t p) -> p t", p=P)).then_inc(consts_in, 16)
            step(pool.memset(ident[:, :], 0.0))
            pool.affine_select(out=ident[:, :], in_=ident[:, :], compare_op=ALU.not_equal, fill=1.0, base=0,
                               pattern=[[-1, P]], channel_multiplier=1).then_inc(ident_ready, 1)
            step(pool.memset(causal[:, :], 1))
            step(pool.affine_select(out=causal[:, :], in_=causal[:, :], compare_op=ALU.is_ge, fill=0.0,
                                    base=0, pattern=[[1, P]], channel_multiplier=-1))
            pool.memset(minus_half[:, :], -0.5)
            for i in range(HALF):
                last = pool.memset(freq[:, i:i + 1], float(ROPE_BASE ** (-2.0 * i / ROPE)))
            step(last)
            for b in range(NB):
                pool.wait_ge(ssq_ready, b + 1)
                rsqrt(rstd[:, 0, b:b + 1], ssq[:, 0, b:b + 1], D, rstd_ready)
                if b < KT:
                    low_part(0, b)
            pool.wait_ge(xn_ready, NB)
            pool.dma_start(gqk[:, 0, :], q_head_norm[0].partition_broadcast(P)).then_inc(phase_in, 16)
            pool.dma_start(gqk[:, 1, :], k_head_norm[0].partition_broadcast(P)).then_inc(phase_in, 16)
            pool.dma_start(gn[:, :], gla_out_norm[0].partition_broadcast(P)).then_inc(phase_in, 16)
            pool.dma_start(wgate[:, :], w_gate_up[0]).then_inc(phase_in, 16)
            for q in range(1, IN_GROUPS):
                for k in range(KT):
                    low_part(q, k)

            pool.wait_ge(z_ready, NB * IN_GROUPS)
            pool.memset(ones[:, :], 1.0).then_inc(sc_zero, 1)
            for t in range(GT):
                pool.wait_ge(g_exp, 4 * t + 3)
                pool.tensor_tensor(g_ke[:, t, :], g_ke[:, t, :], g_k[:, t, :], ALU.mult).then_inc(ke_ready, 1)
                pool.wait_ge(g_exp, 4 * t + 4)
                pool.tensor_tensor(g_qf[:, t, :], g_qf[:, t, :], g_q[:, t, :], ALU.mult).then_inc(qf_ready, 1)
            pool.wait_ge(qs_ready, 2 * GT)
            pool.wait_ge(ke_ready, GT)
            pool.wait_ge(qf_ready, GT)
            pool.memset(sc[:, :, :, :], 0.0).then_inc(sc_zero, 1)
            pool.memset(state[:, :, :, :], 0.0).then_inc(sc_zero, 1)
            pool.wait_ge(c_ss_ready, 2 * NB)
            step(pool.tensor_scalar(c_rs[:, 0, :], c_ss[:, 0, :], 1.0 / QR, EPS, ALU.mult, ALU.add))
            step(pool.tensor_scalar(c_rs[:, 1, :], c_ss[:, 1, :], 1.0 / KVR, EPS, ALU.mult, ALU.add))
            for i in range(2):
                pool.tensor_tensor(c_rs[:, i, :], c_rs[:, i, :], minus_half[:, 0:NB],
                                   ALU.pow).then_inc(c_rs_ready, 1)
            for b in range(NB):
                pool.wait_ge(g_ss_ready, b + 1)
                rsqrt(g_rs[:, b % 2, :], g_ss[:, b % 2, :], GDV, g_rs_ready)
            step(pool.tensor_scalar(gqk[:, 0, :], gqk[:, 0, :], SCALE, None, ALU.mult))

            def heads(b):
                qk = m_qk[:, b % 2, :, :]
                if b >= 2:
                    pool.wait_ge(job_ready, NJOB * (b - 1))
                if b == 0:
                    pool.wait_ge(o_ready, NB)
                step(pool.tensor_copy(qk[:, MH:2 * MH, NOPE:DQK],
                                      zm[:, b, QR + KVR:MLA_W].unsqueeze(1).broadcast_to([P, MH, ROPE])))
                pool.wait_ge(job_out, NJOB * b + 5)
                pool.tensor_tensor(m_sq[:, :, :], qk, qk, ALU.mult).then_inc(sq_ready, 1)
                pool.wait_ge(h_ss_ready, b + 1)
                step(pool.tensor_scalar(h_rs[:, :], h_ss[:, :], 1.0 / DQK, EPS, ALU.mult, ALU.add))
                step(pool.tensor_tensor(h_rs[:, :], h_rs[:, :], minus_half[:, :], ALU.pow))
                step(pool.tensor_tensor(qk, qk, h_rs[:, :].unsqueeze(2).broadcast_to([P, 2 * MH, DQK]), ALU.mult))
                for i in range(2):
                    part = qk[:, i * MH:(i + 1) * MH, :]
                    last = pool.tensor_tensor(part, part, gqk[:, i:i + 1, :].broadcast_to([P, MH, DQK]), ALU.mult)
                step(last)
                pe = qk[:, :, NOPE:DQK].rearrange("p h (a i) -> p h a i", a=2)
                c = cos[:, b, :].unsqueeze(1).unsqueeze(1).broadcast_to([P, 2 * MH, 2, HALF])
                s = sin[:, b, :].unsqueeze(1).unsqueeze(1).broadcast_to([P, 2 * MH, 2, HALF])
                pool.tensor_tensor(m_rc[:, :, :, :], pe, c, ALU.mult)
                step(pool.tensor_tensor(m_rs[:, :, :, :], pe, s, ALU.mult))
                pool.tensor_tensor(pe[:, :, 0, :], m_rc[:, :, 0, :], m_rs[:, :, 1, :], ALU.subtract)
                pool.tensor_tensor(pe[:, :, 1, :], m_rs[:, :, 0, :], m_rc[:, :, 1, :],
                                   ALU.add).then_inc(qk_ready, 1)

            pool.wait_ge(rope_ready, 2)
            for b in range(NB):
                heads(b)
            pool.dma_start(gain[:, :], mlp_norm[0].partition_broadcast(P)).then_inc(gain_in, 16)
            for q in range(IN_GROUPS, Q_UP):
                for k in range(KT):
                    low_part(q, k)
            for k in range(KT):
                low_part_at(0, KT * Q_UP, k)
            for b in range(NB):
                pool.wait_ge(ssq_ready, NB + b + 1)
                rsqrt(rstd[:, 1, b:b + 1], ssq[:, 1, b:b + 1], D, rstd_ready)
            for k in range(KT):
                low_part_at(1, KT * (Q_UP + 1), k)
            with pool.Fori(1, FG) as g:
                for half in range(2):
                    for k in range(KT):
                        low_part_at(half, KT * (Q_UP + half) + 2 * KT * g, k)

        @block.scalar
        def _(act):
            steps = [0]

            def step(ins):
                steps[0] += 1
                ins.then_inc(act_step, 1)
                act.wait_ge(act_step, steps[0])

            def copy(dst, src, scale=1.0):
                return act.activation(dst, src, ACT.Copy, scale=scale)

            def high_part(q, k):
                width = ZM if q == 0 else W
                act.wait_ge(raw_in[k % RING], raw_value(q, k))
                copy(w_hi[:, q % 2, k, 0:width], raw[:, k % RING, 0:width]).then_inc(whi_done, 1)

            def high_part_at(half, g, k):
                act.wait_ge(raw_in[k % RING], 16 * (2 * (Q_UP + half) + k // RING + 1) + 32 + 64 * g)
                copy(w_hi[:, half, k, :], raw[:, k % RING, :]).then_inc(whi_done, 1)

            def square_x(r, b):
                if NB * r + b:
                    act.wait_ge(ssq_ready, NB * r + b)
                act.activation(ps[:, 6:8, :].rearrange("p a n -> p (a n)"), xs[:, b, :], ACT.Square,
                               accum_out=ssq[:, r, b:b + 1]).then_inc(ssq_ready, 1)

            def norm_hi(r, b):
                for j in range(2):
                    n = 2 * (NB * r + b) + j
                    act.wait_ge(xT_ready, n + 1)
                    copy(a_hi[:, 4 * j:4 * j + 4, b * P:(b + 1) * P], bank4(4 + j)).then_inc(ahi_done, 1)

            for b in range(NB):
                act.dma_start(xs[:, b, :], x_d[b]).then_inc(x_in[b], 16)
            for b in range(NB):
                act.wait_ge(x_in[b], 16)
                square_x(0, b)
                high_part(0, b)
                if b >= 1:
                    norm_hi(0, b - 1)
            norm_hi(0, NB - 1)
            act.wait_ge(rope_arg, 1)
            act.activation(sin[:, :, :], sin[:, :, :], ACT.Sin).then_inc(rope_ready, 1)
            act.activation(cos[:, :, :], cos[:, :, :], ACT.Sin).then_inc(rope_ready, 1)
            for q in range(1, IN_GROUPS):
                if q >= 2:
                    act.wait_ge(z_ready, NB * (q - 1))
                for k in range(KT):
                    high_part(q, k)

            act.wait_ge(z_ready, NB * IN_GROUPS)
            for b in range(NB):
                act.wait_ge(qkT_ready, b + 1)
                copy(g_q[:, :, b * P:(b + 1) * P], bank4(4 + b % 4)[:, 0:GT, :], float(GDK) ** -0.5)
                copy(g_k[:, :, b * P:(b + 1) * P], bank4(4 + b % 4)[:, GT:2 * GT, :]).then_inc(qkT_out, 1)
            for t in range(GT):
                act.wait_ge(logit_out, 2 * t + 2)
                step(act.activation(g_cum[:, t, :], g_log[:, t, :], ACT.Abs))
                step(act.activation(g_cum[:, t, :], g_cum[:, t, :], ACT.Exp, scale=-1.0))
                act.activation(g_cum[:, t, :], g_cum[:, t, :], ACT.Ln, bias=1.0).then_inc(softplus_ready, 1)
            for t in range(GT):
                act.wait_ge(from_mid, t + 1)
                act.activation(g_ks[:, t, :], g_qs[:, t, :], ACT.Exp, scale=-1.0).then_inc(g_exp, 1)
                act.wait_ge(g_exp, 4 * t + 1)
                act.activation(g_qs[:, t, :], g_qs[:, t, :], ACT.Exp).then_inc(g_exp, 1)
                act.wait_ge(to_last, t + 1)
                act.activation(g_ke[:, t, :], g_ke[:, t, :], ACT.Exp).then_inc(g_exp, 1)
                ends = g_cum[:, t, :].rearrange("p (b c) -> p b c", c=P)[:, :, P - 1]
                act.activation(decay[:, t, :], ends, ACT.Exp)
                act.activation(g_qf[:, t, :], g_cum[:, t, :], ACT.Exp).then_inc(g_exp, 1)
            act.wait_ge(z_out, NB * IN_GROUPS)
            for b in range(NB):
                act.activation(tanh_g[:, b, :], zg[:, b, :], ACT.Tanh, scale=0.5).then_inc(tanh_ready, 1)
            for b in range(NB):
                if b:
                    act.wait_ge(c_ss_ready, 2 * b)
                act.activation(ps[:, 7, 0:QR], zm[:, b, 0:QR], ACT.Square,
                               accum_out=c_ss[:, 0, b:b + 1]).then_inc(c_ss_ready, 1)
                act.wait_ge(c_ss_ready, 2 * b + 1)
                act.activation(ps[:, 7, 0:KVR], zm[:, b, QR:QR + KVR], ACT.Square,
                               accum_out=c_ss[:, 1, b:b + 1]).then_inc(c_ss_ready, 1)
            for b in range(NB):
                act.wait_ge(keT_ready, b + 1)
                copy(ke_tok[:, b, :], ps[:, b % 4, 0:GH * GDK]).then_inc(keT_out, 1)

            def gla_mix_hi(b):
                act.wait_ge(ogT_ready, b + 1)
                copy(a_hi[:, 0:GH, b * P:(b + 1) * P], bank4(2)).then_inc(g_mix_hi, 1)

            act.wait_ge(qs_ready, 2 * GT)
            act.wait_ge(ke_ready, GT)
            for b in range(NB):
                act.wait_ge(o_ready, b + 1)
                if b >= 2:
                    act.wait_ge(g_ss_ready, b - 1)
                act.activation(osq[:, b % 2, :, :], bank4(b % 2), ACT.Square).then_inc(osq_ready, 1)
                if b >= 1:
                    gla_mix_hi(b - 1)
            gla_mix_hi(NB - 1)

            def job(b, j):
                act.wait_ge(job_ready, NJOB * b + j + 1)
                blk = slice(b * P, (b + 1) * P)
                bank = ps[:, 7, :]
                if j == 0:
                    for i in range(3):
                        last = copy(m_cT[:, b % 2, i, :], bank[:, i * P:(i + 1) * P], ga[:, i:i + 1])
                elif j <= 2:
                    h = 4 * (j - 1)
                    last = copy(m_qk[:, b % 2, h:h + 4, :], bank[:, 0:4 * DQK].rearrange("p (h d) -> p h d", d=DQK))
                elif j <= 4:
                    h = 4 * (j - 3)
                    kv = bank4(7)
                    copy(m_qk[:, b % 2, MH + h:MH + h + 4, 0:NOPE], kv[:, :, 0:NOPE])
                    last = copy(m_v[:, b, h * MV:(h + 4) * MV].rearrange("p (h d) -> p h d", d=MV), kv[:, :, NOPE:NOPE + MV])
                elif j <= 6:
                    h = 4 * (j - 5)
                    last = copy(m_qT[:, b % 2, h:h + 4, :], bank4(7, DQK))
                else:
                    h = 4 * (j - 7)
                    last = copy(m_kT[:, h:h + 4, blk], bank4(7, DQK))
                last.then_inc(job_out, 1)

            def exp(i):
                b, h = STEPS[i]
                nk = (b + 1) * P
                act.wait_ge(max_ready, i + 1)
                if i >= 2:
                    act.wait_ge(pT_ready, 2 * (i - 1))
                act.activation(m_p[:, i % 2, 0:nk], ps[:, 2 * (i % 2):2 * (i % 2) + 2, :].rearrange("p a n -> p (a n)")[:, 0:nk],
                               ACT.Exp, bias=m_nm[:, i % 2:i % 2 + 1],
                               accum_out=m_sum[:, i % 2:i % 2 + 1]).then_inc(p_ready, 1)

            act.wait_ge(z_ready, NB * IN_GROUPS)
            act.wait_ge(consts_in, 64)
            act.wait_ge(g_mix_lo, NB)
            for j in range(NJOB):
                job(0, j)
            exp(0)
            for i, (b, h) in enumerate(STEPS):
                if i + 1 < len(STEPS):
                    exp(i + 1)
                act.wait_ge(pT_ready, 2 * i + 1)
                if i >= 2:
                    act.wait_ge(pv_done, i - 1)
                n = min(b + 1, 4)
                copy(m_pT[:, i % 2, 0:n, :], bank4(4)[:, 0:n, :]).then_inc(pT_out, 1)
                if b + 1 < NB:
                    for j in JOBS.get(h, ()):
                        job(b + 1, j)
                if h == 0 and b >= 1:
                    act.wait_ge(pv_done, MH * b)
                    copy(a_hi[:, GH:KT, (b - 1) * P:b * P], bank4(6)).then_inc(m_mix_hi, 1)
            act.wait_ge(pv_done, len(STEPS))
            copy(a_hi[:, GH:KT, T - P:T], bank4(6)).then_inc(m_mix_hi, 1)

            for q in range(IN_GROUPS, Q_UP):
                for k in range(KT):
                    high_part(q, k)
            act.wait_ge(z_ready, NB * (IN_GROUPS + 1))
            for k in range(KT):
                high_part_at(0, 0, k)
            for b in range(NB):
                act.wait_ge(z_out, NB * (Q_UP - 1) + b + 1)
                square_x(1, b)
                if b >= 1:
                    norm_hi(1, b - 1)
            norm_hi(1, NB - 1)
            act.wait_ge(z_ready, NB * Q_UP)
            for k in range(KT):
                high_part_at(1, 0, k)
            act.sem_inc(up_bank_free, 4)

            def group(g, last):
                for j in range(2 * FT):
                    f, half = j // 2, j % 2
                    act.wait_ge(up_ready, 2 * FT * g + j + 1)
                    if j >= 2:
                        act.wait_ge(actlo_done, 2 * FT * g + j - 1)
                    act.activation(relu[:, j % 2, :], ps[:, j % 4, :], ACT.Relu).then_inc(up_bank_free, 1)
                    act.wait_ge(up_bank_free, 4 + 2 * FT * g + j + 1)
                    act.activation(act_hi[:, f, half * W:(half + 1) * W], relu[:, j % 2, :],
                                   ACT.Square).then_inc(acthi_done, 1)
                if not last:
                    for k in range(KT):
                        high_part_at(0, g + 1, k)
                    act.wait_ge(y_ready, 2 * NB * g + 2 * NB)
                    for k in range(KT):
                        high_part_at(1, g + 1, k)

            with act.Fori(0, FG - 1) as g:
                group(g, False)
            group(FG - 1, True)

        @block.vector
        def _(dve):
            steps = [0]

            def step(ins):
                steps[0] += 1
                ins.then_inc(dve_step, 1)
                dve.wait_ge(dve_step, steps[0])

            def stt(out_, in0, scalar, in1, op0, op1):
                return dve.scalar_tensor_tensor(out=out_, in0=in0, scalar=scalar, in1=in1, op0=op0, op1=op1)

            def norm_x(r, b, dst):
                dve.wait_ge(rstd_ready, NB * r + b + 1)
                stt(dst, xs[:, b, :], rstd[:, r, b:b + 1], gain[:, :], ALU.mult, ALU.mult).then_inc(xn_ready, 1)

            def norm_lo(r, b):
                for j in range(2):
                    n = 2 * (NB * r + b) + j
                    blk = slice(b * P, (b + 1) * P)
                    dve.wait_ge(ahi_done, n + 1)
                    dve.tensor_tensor(a_lo[:, 4 * j:4 * j + 4, blk], bank4(4 + j),
                                      a_hi[:, 4 * j:4 * j + 4, blk].bitcast(F32), ALU.subtract).then_inc(alo_done, 1)

            dve.wait_ge(gain_in, 16)
            for b in range(NB):
                norm_x(0, b, xs[:, b, :])
                if b >= 1:
                    norm_lo(0, b - 1)
            norm_lo(0, NB - 1)
            dve.wait_ge(consts_in, 64)
            dve.wait_ge(pool_step, 4)
            step(dve.tensor_copy(rk[:, :, 0], pos[:, :]))
            for i in range(1, HALF):
                last = dve.tensor_scalar(rk[:, :, i], rk[:, :, 0], freq[:, i:i + 1], None, ALU.mult)
            step(last)
            for table, quarter in ((sin, 0.0), (cos, 0.25)):
                step(dve.tensor_scalar(table[:, :, :], rk[:, :, :], 1.0 / TWO_PI, quarter, ALU.mult, ALU.add))
                step(dve.tensor_scalar(table[:, :, :], table[:, :, :], ROUND, -ROUND, ALU.add, ALU.add))
                step(stt(rt[:, :, :], table[:, :, :], -TWO_PI_A, rk[:, :, :], ALU.mult, ALU.add))
                step(stt(rt[:, :, :], table[:, :, :], -TWO_PI_B, rt[:, :, :], ALU.mult, ALU.add))
                step(stt(rt[:, :, :], table[:, :, :], -TWO_PI_C, rt[:, :, :], ALU.mult, ALU.add))
                step(dve.tensor_scalar(rt[:, :, :], rt[:, :, :], quarter * TWO_PI, PI_SAFE, ALU.add, ALU.min))
                last = dve.tensor_scalar(table[:, :, :], rt[:, :, :], -PI_SAFE, None, ALU.max)
                if quarter:
                    last.then_inc(rope_arg, 1)
                else:
                    step(last)
            dve.wait_ge(rope_arg, 1)
            dests = [lambda b: zm[:, b, :], lambda b: zqk[:, b, :], lambda b: zv[:, b, :], lambda b: zg[:, b, :]]
            for q in range(IN_GROUPS):
                for b in range(NB):
                    n = NB * q + b
                    dve.wait_ge(z_ready, n + 1)
                    width = ZM if q == 0 else W
                    dve.tensor_copy(dests[q](b), ps[:, n % 4, 0:width]).then_inc(z_out, 1)

            dve.wait_ge(gateT_ready, 1)
            for i in range(2):
                dve.tensor_copy(zgateT[:, i * W:(i + 1) * W], ps[0:GR, i, :]).then_inc(gateT_out, 1)
            for t in range(GT):
                for i in range(2):
                    n = 2 * t + i
                    dve.wait_ge(logit_ready, n + 1)
                    dve.tensor_scalar(g_log[:, t, i * W:(i + 1) * W], ps[:, n, :], bg[:, t:t + 1], None,
                                      ALU.add).then_inc(logit_out, 1)
            dve.wait_ge(sc_zero, 1)

            def blocks(a):
                return a.rearrange("p (b c) -> p b c", c=P)

            for t in range(GT):
                dve.wait_ge(softplus_ready, t + 1)
                step(stt(g_log[:, t, :], g_log[:, t, :], 0.0, g_cum[:, t, :], ALU.min, ALU.subtract))
                step(dve.tensor_scalar(g_log[:, t, :], g_log[:, t, :], 1.0 / GATE_NORM, LOG_GATE_MIN, ALU.mult, ALU.max))
                for b in range(NB):
                    blk = slice(b * P, (b + 1) * P)
                    last = dve.tensor_tensor_scan(g_cum[:, t, blk], ones[:, :], g_log[:, t, blk], 0.0, ALU.mult, ALU.add)
                step(last)
                cum = blocks(g_cum[:, t, :])
                mid = cum[:, :, CHUNK - 1:CHUNK].broadcast_to([P, NB, P])
                end = cum[:, :, P - 1:P].broadcast_to([P, NB, P])
                dve.tensor_tensor(blocks(g_qs[:, t, :]), cum, mid, ALU.subtract).then_inc(from_mid, 1)
                dve.tensor_tensor(blocks(g_ke[:, t, :]), end, cum, ALU.subtract).then_inc(to_last, 1)
            for t in range(GT):
                dve.wait_ge(g_exp, 4 * t + 2)
                dve.tensor_tensor(g_qs[:, t, :], g_qs[:, t, :], g_q[:, t, :], ALU.mult).then_inc(qs_ready, 1)
                dve.tensor_tensor(g_ks[:, t, :], g_ks[:, t, :], g_k[:, t, :], ALU.mult).then_inc(qs_ready, 1)
            dve.wait_ge(phase_in, 64)
            for b in range(NB):
                dve.wait_ge(tanh_ready, b + 1)
                step(stt(zg[:, b, :], tanh_g[:, b, :], 1.0, zg[:, b, :], ALU.add, ALU.mult))
                g4 = zg[:, b, :].rearrange("p (h v) -> p h v", h=GH)
                stt(g4, g4, 0.5, gn[:, :].unsqueeze(1).broadcast_to([P, GH, GDV]), ALU.mult, ALU.mult).then_inc(zg_ready, 1)
            dve.wait_ge(sc_zero, 3)

            def gla_mask(b):
                dve.wait_ge(scT_ready, b + 1)
                if b >= 2:
                    dve.wait_ge(o_ready, b - 1)
                for s in range(2):
                    last = dve.copy_predicated(sc[:, b % 2, s::2, :], causal[:, :].unsqueeze(1).broadcast_to([P, GT, P]),
                                               bank4(4 + 2 * (b % 2) + s)[:, 0:GT, :])
                last.then_inc(sc_ready, 1)

            def gla_out(b):
                dve.wait_ge(osq_ready, b + 1)
                dve.tensor_reduce(g_ss[:, b % 2, :], osq[:, b % 2, :, :], AX.X, ALU.add).then_inc(g_ss_ready, 1)
                dve.wait_ge(g_rs_ready, b + 1)
                if b >= 2:
                    dve.wait_ge(ogT_ready, b - 1)
                step(dve.tensor_tensor(og[:, b % 2, :, :], bank4(b % 2),
                                       g_rs[:, b % 2, :].unsqueeze(2).broadcast_to([P, GH, GDV]), ALU.mult))
                g4 = zg[:, b, :].rearrange("p (h v) -> p h v", h=GH)
                dve.tensor_tensor(og[:, b % 2, :, :], og[:, b % 2, :, :], g4, ALU.mult).then_inc(og_ready, 1)

            def gla_lo(b):
                blk = slice(b * P, (b + 1) * P)
                dve.wait_ge(g_mix_hi, b + 1)
                dve.tensor_tensor(a_lo[:, 0:GH, blk], bank4(2), a_hi[:, 0:GH, blk].bitcast(F32),
                                  ALU.subtract).then_inc(g_mix_lo, 1)

            dve.wait_ge(zg_ready, NB)
            gla_mask(0)
            for b in range(NB):
                if b + 1 < NB:
                    gla_mask(b + 1)
                    dve.wait_ge(kv_ready, b + 1)
                    if b >= 1:
                        dve.wait_ge(o_ready, b)
                        dve.wait_ge(state_ready, b)
                    for t in range(GT):
                        for s in range(2):
                            rows = slice(s * GDK, (s + 1) * GDK)
                            kv = ps[rows, 3, (2 * t + s) * GDV:(2 * t + s + 1) * GDV]
                            own = slice(s * GDV, (s + 1) * GDV)
                            last = stt(state[rows, (b + 1) % 2, t, own], state[rows, b % 2, t, own],
                                       decay[rows, t, b:b + 1], kv, ALU.mult, ALU.add)
                    last.then_inc(state_ready, 1)
                gla_out(b)
                if b >= 1:
                    gla_lo(b - 1)
            gla_lo(NB - 1)

            dve.wait_ge(c_rs_ready, 2)
            for b in range(NB):
                dve.tensor_scalar(zm[:, b, 0:QR], zm[:, b, 0:QR], c_rs[:, 0, b:b + 1], None, ALU.mult)
                dve.tensor_scalar(zm[:, b, QR:QR + KVR], zm[:, b, QR:QR + KVR], c_rs[:, 1, b:b + 1], None,
                                  ALU.mult).then_inc(c_ready, 1)

            def head_sums(b):
                dve.wait_ge(sq_ready, b + 1)
                dve.tensor_reduce(h_ss[:, :], m_sq[:, :, :], AX.X, ALU.add).then_inc(h_ss_ready, 1)

            def row_max(i):
                b, h = STEPS[i]
                nk = (b + 1) * P
                s = ps[:, 2 * (i % 2):2 * (i % 2) + 2, :].rearrange("p a n -> p (a n)")
                dve.wait_ge(s_ready, i + 1)
                step(dve.memset(s[0:CHUNK, nk - CHUNK:nk], MASKED))
                dve.tensor_reduce(m_nm[:, i % 2:i % 2 + 1], s[:, 0:nk], AX.X, ALU.max, negate=True).then_inc(max_ready, 1)

            def normalise(i):
                b, h = STEPS[i]
                nk = (b + 1) * P
                dve.wait_ge(p_ready, i + 1)
                step(dve.reciprocal(m_rden[:, i % 2:i % 2 + 1], m_sum[:, i % 2:i % 2 + 1]))
                dve.tensor_scalar(m_p[:, i % 2, 0:nk], m_p[:, i % 2, 0:nk], m_rden[:, i % 2:i % 2 + 1], None,
                                  ALU.mult).then_inc(pn_ready, 1)

            def mla_lo(b):
                blk = slice(b * P, (b + 1) * P)
                dve.wait_ge(m_mix_hi, b + 1)
                dve.tensor_tensor(a_lo[:, GH:KT, blk], bank4(6), a_hi[:, GH:KT, blk].bitcast(F32),
                                  ALU.subtract).then_inc(m_mix_lo, 1)

            head_sums(0)
            row_max(0)
            row_max(1)
            normalise(0)
            for i, (b, h) in enumerate(STEPS):
                if h == 4 and b + 1 < NB:
                    head_sums(b + 1)
                if i + 2 < len(STEPS):
                    row_max(i + 2)
                if i + 1 < len(STEPS):
                    normalise(i + 1)
                if b >= 4:
                    dve.wait_ge(pT_ready, 2 * i + 2)
                    if i >= 2:
                        dve.wait_ge(pv_done, i - 1)
                    dve.tensor_copy(m_pT[:, i % 2, 4:b + 1, :], bank4(5)[:, 0:b - 3, :]).then_inc(pT_out2, 1)
                if h == 0 and b >= 1:
                    mla_lo(b - 1)
            mla_lo(NB - 1)

            def residual(n, b):
                m = NB * (IN_GROUPS + n) + b
                dve.wait_ge(z_ready, m + 1)
                if n == 0:
                    dve.wait_ge(x_in[b], 32)
                xh = xs[:, b, n * W:(n + 1) * W]
                dve.tensor_tensor(xh, ps[:, m % 4, :], xh, ALU.add).then_inc(z_out, 1)

            for b in range(NB):
                residual(0, b)
            dve.wait_ge(gain_in, 32)
            for b in range(NB):
                residual(1, b)
                if b >= 1:
                    if b - 1 >= 2:
                        dve.wait_ge(xT_ready, 2 * (NB + b - 2))
                    norm_x(1, b - 1, xn2[:, (b - 1) % 2, :])
                if b >= 2:
                    norm_lo(1, b - 2)
            dve.wait_ge(xT_ready, 2 * (NB + NB - 2))
            norm_x(1, NB - 1, xn2[:, (NB - 1) % 2, :])
            norm_lo(1, NB - 2)
            norm_lo(1, NB - 1)
            dve.sem_inc(y_bank_free, 4)

            def group(g):
                for j in range(2 * FT):
                    f, half = j // 2, j % 2
                    cols = slice(half * W, (half + 1) * W)
                    dve.wait_ge(acthi_done, 2 * FT * g + j + 1)
                    dve.tensor_tensor(relu[:, j % 2, :], relu[:, j % 2, :], relu[:, j % 2, :],
                                      ALU.mult).then_inc(relu_ready, 1)
                    dve.wait_ge(relu_ready, 2 * FT * g + j + 1)
                    dve.tensor_tensor(act_lo[:, f, cols], relu[:, j % 2, :], act_hi[:, f, cols].bitcast(F32),
                                      ALU.subtract).then_inc(actlo_done, 1)
                for t in range(2 * NB):
                    b, n = t // 2, t % 2
                    dve.wait_ge(y_ready, 2 * NB * g + t + 1)
                    xh = xs[:, b, n * W:(n + 1) * W]
                    dve.tensor_tensor(xh, ps[:, 4 + t % 4, :], xh, ALU.add).then_inc(y_bank_free, 1)

            with dve.Fori(0, FG) as g:
                group(g)

        @block.tensor
        def _(pe):
            def mm(dst, lhsT, rhs, start, stop):
                return pe.matmul(dst, lhsT, rhs, start=start, stop=stop)

            def split_product(dst, hi, lo, rhs_hi, rhs_lo, first, last):
                mm(dst, hi, rhs_hi, first, False)
                mm(dst, hi, rhs_lo, False, False)
                return mm(dst, lo, rhs_hi, False, last)

            def norm_T(r, b, src):
                pe.wait_ge(xn_ready, NB * r + b + 1)
                for j in range(2):
                    n = 2 * (NB * r + b) + j
                    if n >= 2:
                        pe.wait_ge(alo_done, n - 1)
                    for i in range(4):
                        last = pe.transpose(bank4(4 + j)[:, i, :], src[:, (4 * j + i) * P:(4 * j + i + 1) * P], ident[:, :])
                    last.then_inc(xT_ready, 1)

            def project(q, b):
                n = NB * q + b
                blk = slice(b * P, (b + 1) * P)
                width = ZM if q == 0 else W
                if n >= 4:
                    pe.wait_ge(z_out, n - 3)
                for k in range(KT):
                    if b == 0:
                        pe.wait_ge(wlo_done, KT * q + k + 1)
                    last = split_product(ps[:, n % 4, 0:width], a_hi[:, k, blk], a_lo[:, k, blk],
                                         w_hi[:, q % 2, k, 0:width], w_lo[:, q % 2, k, 0:width], k == 0, k == KT - 1)
                last.then_inc(z_ready, 1)

            pe.wait_ge(ident_ready, 1)
            for b in range(NB):
                norm_T(0, b, xs[:, b, :])
            for b in range(NB):
                pe.wait_ge(alo_done, 2 * b + 2)
                project(0, b)
            for q in range(1, IN_GROUPS):
                for b in range(NB):
                    project(q, b)

            for b in range(NB):
                if b >= 4:
                    pe.wait_ge(qkT_out, b - 3)
                for i in range(2 * GT):
                    last = pe.transpose(bank4(4 + b % 4)[:, i, :], zqk[:, b, i * P:(i + 1) * P], ident[:, :])
                last.then_inc(qkT_ready, 1)
            pe.wait_ge(z_out, NB * IN_GROUPS)
            for b in range(NB):
                last = pe.transpose(bank4(b // 4, GR)[:, b % 4, :], zm[:, b, MLA_W:ZM], ident[:, :])
            last.then_inc(gateT_ready, 1)
            pe.wait_ge(phase_in, 64)
            pe.wait_ge(gateT_out, 2)
            for t in range(GT):
                for i in range(2):
                    mm(ps[:, 2 * t + i, :], wgate[:, t * P:(t + 1) * P], zgateT[:, i * W:(i + 1) * W],
                       True, True).then_inc(logit_ready, 1)
            pe.wait_ge(logit_out, 4)
            pe.wait_ge(ke_ready, GT)
            for b in range(NB):
                if b >= 4:
                    pe.wait_ge(keT_out, b - 3)
                for t in range(GT):
                    last = pe.transpose(ps[:, b % 4, t * P:(t + 1) * P], g_ke[:, t, b * P:(b + 1) * P], ident[:, :])
                last.then_inc(keT_ready, 1)

            def gla_scores(b):
                if b >= 2:
                    pe.wait_ge(sc_ready, b - 1)
                for h in range(GH):
                    rows = slice((h % 2) * GDK, (h % 2 + 1) * GDK)
                    last = mm(bank4(4 + 2 * (b % 2) + h % 2)[:, h // 2, :], g_ks[rows, h // 2, b * P:(b + 1) * P],
                              g_qs[rows, h // 2, b * P:(b + 1) * P], True, True)
                last.then_inc(scT_ready, 1)

            def gla_mix_T(b):
                pe.wait_ge(og_ready, b + 1)
                if b >= 1:
                    pe.wait_ge(g_mix_lo, b)
                for h in range(GH):
                    last = pe.transpose(bank4(2)[:, h, :], og[:, b % 2, h, :], ident[:, :])
                last.then_inc(ogT_ready, 1)

            pe.wait_ge(qs_ready, 2 * GT)
            pe.wait_ge(qf_ready, GT)
            pe.wait_ge(keT_out, NB)
            gla_scores(0)
            for b in range(NB):
                if b + 1 < NB:
                    gla_scores(b + 1)
                    if b >= 1:
                        pe.wait_ge(state_ready, b)
                    for t in range(GT):
                        last = mm(ps[:, 3, 2 * t * GDV:2 * (t + 1) * GDV], ke_tok[:, b, t * P:(t + 1) * P],
                                  zv[:, b, 2 * t * GDV:2 * (t + 1) * GDV], True, True)
                    last.then_inc(kv_ready, 1)
                if b >= 1:
                    gla_mix_T(b - 1)
                pe.wait_ge(sc_ready, b + 1)
                if b == 0:
                    pe.wait_ge(sc_zero, 3)
                else:
                    pe.wait_ge(state_ready, b)
                if b >= 2:
                    pe.wait_ge(og_ready, b - 1)
                for t in range(GT):
                    mm(ps[:, b % 2, 2 * t * GDV:2 * (t + 1) * GDV], g_qf[:, t, b * P:(b + 1) * P],
                       state[:, b % 2, t, :], True, False)
                    for h in (2 * t, 2 * t + 1):
                        last = mm(bank4(b % 2)[:, h, :], sc[:, b % 2, h, :], zv[:, b, h * GDV:(h + 1) * GDV],
                                  False, h % 2 == 1)
                last.then_inc(o_ready, 1)
            gla_mix_T(NB - 1)

            def job(b, j):
                n = NJOB * b + j
                if n >= 1:
                    pe.wait_ge(job_out, n)
                bank = ps[:, 7, :]
                cT = m_cT[:, b % 2, :, :]
                if j == 0:
                    pe.wait_ge(c_ready, b + 1)
                    for i in range(3):
                        last = pe.transpose(bank[:, i * P:(i + 1) * P], zm[:, b, i * P:(i + 1) * P], ident[:, :])
                elif j <= 2:
                    h = 4 * (j - 1)
                    for i in range(QR // P):
                        last = mm(bank[:, 0:4 * DQK], cT[:, i, :], m_uq[:, i, h * DQK:(h + 4) * DQK],
                                  i == 0, i == QR // P - 1)
                elif j <= 4:
                    c = (j - 3) * W
                    last = mm(bank, cT[:, 2, :], m_ukv[:, c:c + W], True, True)
                else:
                    if j == 5:
                        pe.wait_ge(qk_ready, b + 1)
                    h = 4 * (j - 5)
                    for i in range(4):
                        last = pe.transpose(bank4(7, DQK)[:, i, :], m_qk[:, b % 2, h + i, :], ident[:, :])
                last.then_inc(job_ready, 1)

            def scores(i):
                b, h = STEPS[i]
                nk = (b + 1) * P
                if i >= 2:
                    pe.wait_ge(p_ready, i - 1)
                if h == 0:
                    pe.wait_ge(job_out, NJOB * (b + 1))
                for c in range(0, nk, W):
                    n = min(W, nk - c)
                    last = mm(ps[:, 2 * (i % 2) + c // W, 0:n], m_qT[:, b % 2, h, :], m_kT[:, h, c:c + n], True, True)
                last.then_inc(s_ready, 1)

            def p_transposes(i):
                b, h = STEPS[i]
                pe.wait_ge(pn_ready, i + 1)
                if i >= 1:
                    pe.wait_ge(pT_out, i)
                if i > MH * 4:
                    pe.wait_ge(pT_out2, i - MH * 4)
                for c in range(b + 1):
                    last = pe.transpose(bank4(4 + c // 4)[:, c % 4, :], m_p[:, i % 2, c * P:(c + 1) * P], ident[:, :])
                    if c == min(b, 3):
                        last.then_inc(pT_ready, 1 if b >= 4 else 2)
                if b >= 4:
                    last.then_inc(pT_ready, 1)

            def values(i):
                b, h = STEPS[i]
                pe.wait_ge(pT_out, i + 1)
                if b >= 4:
                    pe.wait_ge(pT_out2, i + 1 - MH * 4)
                if h == 0 and b >= 1:
                    pe.wait_ge(m_mix_lo, b)
                dst = ps[(h % 2) * MV:(h % 2 + 1) * MV, 6, (h // 2) * P:(h // 2 + 1) * P]
                for c in range(b + 1):
                    last = mm(dst, m_v[:, c, h * MV:(h + 1) * MV], m_pT[:, i % 2, c, :], c == 0, c == b)
                last.then_inc(pv_done, 1)

            pe.wait_ge(mla_w_in, 32)
            for j in range(NJOB):
                job(0, j)
            scores(0)
            scores(1)
            for i, (b, h) in enumerate(STEPS):
                if i + 2 < len(STEPS) and h < MH - 2:
                    scores(i + 2)
                p_transposes(i)
                if i >= 1:
                    values(i - 1)
                if b + 1 < NB:
                    for j in JOBS.get(h, ()):
                        job(b + 1, j)
                if i + 2 < len(STEPS) and h >= MH - 2:
                    scores(i + 2)
            values(len(STEPS) - 1)

            pe.wait_ge(m_mix_lo, NB)
            for n in range(NH):
                for b in range(NB):
                    project(IN_GROUPS + n, b)
                    if n == NH - 1 and b >= 2:
                        norm_T(1, b - 2, xn2[:, b % 2, :])
            norm_T(1, NB - 2, xn2[:, NB % 2, :])
            norm_T(1, NB - 1, xn2[:, (NB - 1) % 2, :])

            def group(g, first):
                for j in range(2 * FT):
                    f, half = j // 2, j % 2
                    cols = slice(half * W, (half + 1) * W)
                    pe.wait_ge(up_bank_free, 2 * FT * g + j + 1)
                    for k in range(KT):
                        if j == 0:
                            pe.wait_ge(wlo_done, 2 * KT * g + KT * Q_UP + k + 1)
                        wh = w_hi[:, 0, k, f * P:(f + 1) * P]
                        wl = w_lo[:, 0, k, f * P:(f + 1) * P]
                        last = split_product(ps[:, j % 4, :], wh, wl, a_hi[:, k, cols], a_lo[:, k, cols],
                                             k == 0, k == KT - 1)
                    last.then_inc(up_ready, 1)
                for quad in range(NB // 2):
                    for f in range(FT):
                        pe.wait_ge(actlo_done, 2 * FT * g + 2 * f + quad // 2 + 1)
                        for s in range(4):
                            t = 4 * quad + s
                            b, n = t // 2, t % 2
                            blk = slice(b * P, (b + 1) * P)
                            if f == 0:
                                pe.wait_ge(y_bank_free, 2 * NB * g + t + 1)
                            if quad == 0 and s < 2:
                                pe.wait_ge(wlo_done, 2 * KT * g + KT * (Q_UP + 1) + 2 * f + n + 1)
                            kk = 2 * f + n
                            last = split_product(ps[:, 4 + s, :], act_hi[:, f, blk], act_lo[:, f, blk],
                                                 w_hi[:, 1, kk, :], w_lo[:, 1, kk, :], f == 0, f == FT - 1)
                            if f == FT - 1:
                                last.then_inc(y_ready, 1)

            pe.wait_ge(alo_done, 4 * NB)
            with pe.Fori(0, FG) as g:
                group(g, False)


_INS = ['x', 'positions', 'attn_norm', 'w_in', 'w_gate_up', 'b_gate', 'gla_out_norm', 'q_a_norm', 'w_uq',
        'kv_a_norm', 'w_ukv', 'q_head_norm', 'k_head_norm', 'w_out', 'mlp_norm', 'w_up', 'w_down']


def kernel(**inputs):
    import numpy as _np
    import concourse.bacc as _bacc
    from concourse import mybir as _mybir
    from concourse.bass_utils import run_bass_kernel_spmd as _run

    nc = _bacc.Bacc("TRN2", target_bir_lowering=False, num_devices=1)
    arrays, args = {}, []
    for name in _INS:
        a = _np.ascontiguousarray(inputs[name])
        arrays[f"in_{name}_dram"] = a
        args.append(nc.dram_tensor(f"in_{name}_dram", a.shape, _mybir.dt.from_np(a.dtype), kind="ExternalInput").ap())
    out = nc.dram_tensor("out_0_dram", (1, T, D), F32, kind="ExternalOutput").ap()
    layer(nc, *args, out)
    r = _run(nc, [arrays], core_ids=[0])
    return r.results[0]["out_0_dram"]
```

```python
from contextlib import ExitStack

import concourse.bass as bass
from concourse import mybir

F32 = mybir.dt.float32
F32R = mybir.dt.float32r
I32 = mybir.dt.int32
ALU = mybir.AluOpType
ACT = mybir.ActivationFunctionType
AX = mybir.AxisListType

P = 128
T, D, FF = 1024, 1024, 4096
NB = T // P
KT = D // P
W = 512
NH = D // W
EPS = 1e-6

CHUNK = 64
GH, GDK, GDV, GR = 4, 64, 128, 16
GT = GH * GDK // P
GATE_NORM, LOG_GATE_MIN = 16.0, -1.0

MH, QR, KVR, NOPE, ROPE, MV = 8, 256, 128, 64, 32, 64
DQK = NOPE + ROPE
HALF = ROPE // 2
ROPE_BASE = 10000.0
SCALE = float(DQK) ** -0.5
MASKED = -1e30

C_QK, C_V, C_GATE, C_G, C_MLA = 0, 512, 1024, 1040, 1552
MLA_W = QR + KVR + ROPE
ZM = MLA_W + GR

RING = 4
SLICES = 10
FG = FF // W
FT = W // P
IN_GROUPS, OUT_GROUPS = 4, NH

TWO_PI = 6.283185307179586
TWO_PI_A = 6.28125
TWO_PI_B = 0.0019350051879882812
TWO_PI_C = TWO_PI - TWO_PI_A - TWO_PI_B
ROUND = 12582912.0
PI_SAFE = 3.1415925


def layer(nc, x, positions, attn_norm, w_in, w_gate_up, b_gate, gla_out_norm, q_a_norm, w_uq,
          kv_a_norm, w_ukv, q_head_norm, k_head_norm, w_out, mlp_norm, w_up, w_down, out):
    x_d = x[0].rearrange("(b p) d -> b p d", p=P)
    out_d = out[0].rearrange("(b p) d -> b p d", p=P)
    w_in_d = w_in[0].rearrange("(k p) n -> k p n", p=P)
    w_out_d = w_out[0].rearrange("(k p) (h n) -> h k p n", p=P, n=W)
    w_up_d = w_up[0].rearrange("(k p) (g n) -> g k p n", p=P, n=W)
    w_down_d = w_down[0].rearrange("(g f p) (h n) -> g f h p n", p=P, f=FT, n=W)

    ctx = ExitStack()
    with ctx:
        ctx.enter_context(nc.allow_non_contiguous_dma(reason="gains and positions of a few KB, laid by partition"))

        def sem(name):
            return ctx.enter_context(nc.semaphore(name))

        base = -(-nc.sbuf_base // 64) * 64
        KB = 1024

        def at(name, shape, offset, dt=F32):
            return nc.alloc_sbuf_tensor_at(name, shape, dt, offset=base + offset)

        A, B, X, E, RAW, GB, C = 0, 64 * KB, 128 * KB, 160 * KB, 192 * KB, 200 * KB, 204 * KB
        a_hi = at("a_hi", [P, KT, T], A, F32R)
        a_lo = at("a_lo", [P, KT, T], A + 32 * KB, F32R)
        raw = at("raw", [P, RING, W], RAW)

        x0 = at("x0", [P, NB, D], X)
        gain = at("gain", [P, D], GB)
        wi_hi = at("wi_hi", [P, SLICES, W], B, F32R)
        wi_lo = at("wi_lo", [P, SLICES, W], B + 20 * KB, F32R)
        zqk = at("zqk", [P, NB, W], 104 * KB)
        g_cum = at("g_cum", [P, GT, T], 120 * KB)
        g_log = at("g_log", [P, GT, T], 104 * KB)
        zgateT = at("zgateT", [GR, T], 112 * KB)
        ones = at("ones", [P, P], 116 * KB)
        rk = at("rk", [P, NB, HALF], 117 * KB)
        rt = at("rt", [P, NB, HALF], 117 * KB + 512)
        freq = at("freq", [P, HALF], 118 * KB)
        m_qk = at("m_qk", [P, 2, 2 * MH, DQK], 128 * KB)
        m_sq = at("m_sq", [P, 2 * MH, DQK], 140 * KB)
        m_rc = at("m_rc", [P, 2 * MH, 2, HALF], 140 * KB)
        m_rs = at("m_rs", [P, 2 * MH, 2, HALF], 142 * KB)
        m_uq = at("m_uq", [P, QR // P, MH * DQK], 146 * KB)
        m_ukv = at("m_ukv", [P, MH * (NOPE + MV)], 152 * KB)
        m_cT = at("m_cT", [P, 3, P], 156 * KB)
        q_stage = at("q_stage", [DQK, MH, P], 160 * KB)
        k_stage = at("k_stage", [DQK, MH, P], 164 * KB)
        v_stage = at("v_stage", [P, MH * MV], 168 * KB)
        z_stage = at("z_stage", [P, 2, W], 170 * KB)
        zm = at("zm", [P, NB, ZM], 174 * KB)
        tanh_g = at("tanh_g", [P, W], 188 * KB)
        junk = at("junk", [P, QR], 190 * KB)
        gqk = at("gqk", [P, 2, DQK], GB)
        gn = at("gn", [P, GDV], GB + 768)
        wgate = at("wgate", [GR, GH * GDK], GB + 1280)

        zv = at("zv", [P, NB, W], B)
        zg = at("zg", [P, NB, W], 80 * KB)
        m_p = at("m_p", [P, 2, T], 96 * KB)
        m_v = at("m_v", [P, NB, MH * MV], 128 * KB)
        m_qT = at("m_qT", [DQK, 2, T], 144 * KB)
        m_kT = at("m_kT", [DQK, 2, T], 152 * KB)
        m_pT = at("m_pT", [P, 2, NB, P], 160 * KB)
        g_q, g_k, g_qs, g_ks, g_ke, g_qf = (at(f"g_{name}", [P, 2, GT, P], 168 * KB + 2 * KB * n)
                                            for n, name in enumerate(("q", "k", "qs", "ks", "ke", "qf")))
        sc = at("sc", [P, GH, P], 180 * KB)
        state = at("state", [P, 2, GT, 2 * GDV], 182 * KB)
        og = at("og", [P, GH, GDV], 186 * KB)
        osq = at("osq", [P, GH, GDV], 188 * KB)
        ke_tok = zqk[:, :, 0:GH * GDK]

        w_hi = at("w_hi", [P, 2, KT, W], B, F32R)
        w_lo = at("w_lo", [P, 2, KT, W], B + 32 * KB, F32R)
        xs = at("xs", [P, NB, D], X)
        act_hi = at("act_hi", [P, FT, T], E, F32R)
        act_lo = at("act_lo", [P, FT, T], E + 16 * KB, F32R)
        xn2 = at("xn2", [P, 2, D], E + 24 * KB)
        relu = at("relu", [P, 2, W], GB)

        q_d = nc.dram_tensor("q_heads", (MH, DQK, T), F32, kind="Internal").ap()
        k_d = nc.dram_tensor("k_heads", (MH, DQK, T), F32, kind="Internal").ap()
        v_d = nc.dram_tensor("v_heads", (NB, P, MH * MV), F32, kind="Internal").ap()
        z_d = nc.dram_tensor("z_gla", (2, NB, P, W), F32, kind="Internal").ap()

        place = [C]

        def small(name, shape, dt=F32):
            size = 4
            for n in shape[1:]:
                size *= n
            t = at(name, shape, place[0], dt)
            place[0] += -(-size // 32) * 32
            return t

        ident = small("ident", [P, P])
        causal = small("causal", [P, P], I32)
        cos = small("cos", [P, NB, HALF])
        sin = small("sin", [P, NB, HALF])
        pos = small("pos", [P, NB], I32)
        minus_half = small("minus_half", [P, 2 * MH])
        bg = small("bg", [P, GT])
        ga = small("ga", [P, 3])
        ssq = small("ssq", [P, 2, NB])
        rstd = small("rstd", [P, 2, NB])
        decay = small("decay", [P, GT, NB])
        g_ss = small("g_ss", [P, GH])
        g_rs = small("g_rs", [P, GH])
        c_ss = small("c_ss", [P, NB, 2])
        c_rs = small("c_rs", [P, NB, 2])
        h_ss = small("h_ss", [P, 2 * MH])
        h_rs = small("h_rs", [P, 2 * MH])
        m_nm = small("m_nm", [P, 2])
        m_sum = small("m_sum", [P, 2])
        m_rden = small("m_rden", [P, 2])
        assert base + place[0] <= nc.sbuf_usable_end

        ps = ctx.enter_context(nc.psum_tensor("ps", [P, 8, W], F32))

        def bank4(n, parts=P):
            return ps[0:parts, n, :].rearrange("p (h c) -> p h c", c=P)

        x_in = [sem(f"x_in{b}") for b in range(NB)]
        raw_in = [sem(f"raw_in{s}") for s in range(RING)]
        gain_in, consts_in, phase_in, mla_w_in = sem("gain_in"), sem("consts_in"), sem("phase_in"), sem("mla_w_in")
        stored = sem("stored")
        ident_ready, pool_step, dve_step, act_step = sem("ident_ready"), sem("pool_step"), sem("dve_step"), sem("act_step")
        whi_done, wlo_done = sem("whi_done"), sem("wlo_done")
        ssq_ready, rstd_ready, xn_ready = sem("ssq_ready"), sem("rstd_ready"), sem("xn_ready")
        xT_ready, ahi_done, alo_done = sem("xT_ready"), sem("ahi_done"), sem("alo_done")
        z_ready, z_out = sem("z_ready"), sem("z_out")
        gqk_ready = sem("gqk_ready")
        rope_arg, rope_ready = sem("rope_arg"), sem("rope_ready")
        slice_free = sem("slice_free")
        qkT_ready, qkT_out, gateT_ready, gateT_out = sem("qkT_ready"), sem("qkT_out"), sem("gateT_ready"), sem("gateT_out")
        logit_ready, logit_out, softplus_ready = sem("logit_ready"), sem("logit_out"), sem("softplus_ready")
        from_mid, to_last, g_exp = sem("from_mid"), sem("to_last"), sem("g_exp")
        qs_ready, ke_ready, keT_ready, keT_out = sem("qs_ready"), sem("ke_ready"), sem("keT_ready"), sem("keT_out")
        tanh_ready, ones_ready = sem("tanh_ready"), sem("ones_ready")
        scT_ready, sc_ready, sc_zero, kv_ready, state_ready = sem("scT_ready"), sem("sc_ready"), sem("sc_zero"), sem("kv_ready"), sem("state_ready")
        o_ready, osq_ready, g_ss_ready, g_rs_ready, og_ready = sem("o_ready"), sem("osq_ready"), sem("g_ss_ready"), sem("g_rs_ready"), sem("og_ready")
        ogT_ready, g_mix_hi, g_mix_lo, cum_ready = sem("ogT_ready"), sem("g_mix_hi"), sem("g_mix_lo"), sem("cum_ready")
        qf_ready = sem("qf_ready")
        c_ss_ready, c_rs_ready, c_ready = sem("c_ss_ready"), sem("c_rs_ready"), sem("c_ready")
        cT_ready, cT_out, qkv_ready, qkv_out = sem("cT_ready"), sem("cT_out"), sem("qkv_ready"), sem("qkv_out")
        kpe_ready, sq_ready, h_ss_ready, h_rs_ready, qk_ready = sem("kpe_ready"), sem("sq_ready"), sem("h_ss_ready"), sem("h_rs_ready"), sem("qk_ready")
        headT_ready, qT_out, kT_out = sem("headT_ready"), sem("qT_out"), sem("kT_out")
        q_stored, k_stored, v_stored = sem("q_stored"), sem("k_stored"), sem("v_stored")
        z_stored = [sem(f"z_stored{n}") for n in range(2)]
        head_in = [sem(f"head_in{n}") for n in range(2)]
        v_in = [sem(f"v_in{n}") for n in range(2)]
        zv_in, zg_in = sem("zv_in"), sem("zg_in")
        s_ready, max_ready, p_ready, pn_ready = sem("s_ready"), sem("max_ready"), sem("p_ready"), sem("pn_ready")
        pT_ready, pT_out, pT_out2, pv_done = sem("pT_ready"), sem("pT_out"), sem("pT_out2"), sem("pv_done")
        m_mix_hi, m_mix_lo = sem("m_mix_hi"), sem("m_mix_lo")
        up_ready, up_bank_free, relu_ready = sem("up_ready"), sem("up_bank_free"), sem("relu_ready")
        acthi_done, actlo_done, y_ready, y_bank_free = sem("acthi_done"), sem("actlo_done"), sem("y_ready"), sem("y_bank_free")

        block = ctx.enter_context(nc.Block())

        def raw_value(q, k):
            n = 2 * q + k // RING + 1
            return 16 * n + (16 * (k // RING + 1) if isinstance(q, int) and q == 0 else 32)

        Q_UP = IN_GROUPS + OUT_GROUPS

        def prep(s, first):
            b = (s - first) // 3
            return b if (s - first) % 3 == 0 and 0 <= b < NB else None

        STEPS = [(h, b) for h in range(MH) for b in range(NB)]
        SECOND = NB // 2

        def seconds(i):
            return SECOND * (i // NB) + max(0, i % NB - SECOND)

        def head_out(h, half):
            rows = slice((h % 2) * MV, (h % 2 + 1) * MV)
            return rows, GH + h // 2, slice(half * W, (half + 1) * W)

        POOL_CONSTS = 4

        @block.sync
        def _(sp):
            def piece(q, k, src):
                if not (isinstance(q, int) and q == 0 and k < RING):
                    sp.wait_ge(wlo_done, KT * q + k - RING + 1)
                sp.dma_start(raw[:, k % RING, 0:src.shape[-1]], src).then_inc(raw_in[k % RING], 16)

            def in_piece(q, k):
                if q == 0:
                    piece(0, k, w_in_d[k, :, C_MLA:C_MLA + MLA_W])
                    sp.dma_start(raw[:, k % RING, MLA_W:ZM],
                                 w_in_d[k, :, C_GATE:C_GATE + GR]).then_inc(raw_in[k % RING], 16)
                else:
                    c = (C_V, C_G, C_QK)[q - 1]
                    piece(q, k, w_in_d[k, :, c:c + W])

            for k in range(KT):
                in_piece(0, k)

            def stores(s):
                if NB <= s < 3 * NB:
                    n = s - NB
                    sp.wait_ge(z_out, s + 1)
                    sp.dma_start(z_d[n // NB, n % NB], z_stage[:, n % 2, :]).then_inc(z_stored[n % 2], 16)
                b = prep(s, 8)
                if b is not None:
                    sp.wait_ge(qkv_out, b + 1)
                    sp.dma_start(v_d[b], v_stage[:, :]).then_inc(v_stored, 16)
                b = prep(s, 10)
                if b is not None:
                    blk = slice(b * P, (b + 1) * P)
                    sp.wait_ge(qT_out, b + 1)
                    sp.dma_start(q_d[:, :, blk].rearrange("h d t -> d h t"), q_stage[:, :, :]).then_inc(q_stored, 16)
                    sp.wait_ge(kT_out, b + 1)
                    sp.dma_start(k_d[:, :, blk].rearrange("h d t -> d h t"), k_stage[:, :, :]).then_inc(k_stored, 16)

            for q in range(IN_GROUPS):
                if q + 1 < IN_GROUPS:
                    for k in range(RING + 2):
                        in_piece(q + 1, k)
                if q == 0:
                    sp.wait_ge(alo_done, 2 * NB)
                    sp.dma_start(m_uq[:, :, :], w_uq[0].rearrange("(k p) n -> p k n", p=P)).then_inc(mla_w_in, 16)
                    sp.dma_start(m_ukv[:, :], w_ukv[0]).then_inc(mla_w_in, 16)
                for b in range(NB - 1):
                    stores(NB * q + b)
                if q + 1 < IN_GROUPS:
                    for k in range(RING + 2, KT):
                        in_piece(q + 1, k)
                else:
                    for k in range(RING):
                        piece(IN_GROUPS, k, w_out_d[0, k])
                stores(NB * q + NB - 1)

            def head(h):
                if h >= 2:
                    sp.wait_ge(s_ready, NB * (h - 1))
                sp.dma_start(m_qT[:, h % 2, :], q_d[h]).then_inc(head_in[h % 2], 16)
                sp.dma_start(m_kT[:, h % 2, :], k_d[h]).then_inc(head_in[h % 2], 16)

            sp.wait_ge(q_stored, 16 * NB)
            sp.wait_ge(k_stored, 16 * NB)
            sp.wait_ge(v_stored, 16 * NB)
            head(0)
            for n in range(2):
                half = slice(n * NB // 2, (n + 1) * NB // 2)
                sp.dma_start(m_v[:, half, :], v_d[half].rearrange("b p n -> p b n")).then_inc(v_in[n], 16)
            head(1)
            sp.wait_ge(z_ready, NB * IN_GROUPS)
            for n in range(2):
                sp.wait_ge(z_stored[n], 16 * NB)
            sp.dma_start(zv[:, :, :], z_d[0].rearrange("b p n -> p b n")).then_inc(zv_in, 16)
            sp.dma_start(zg[:, :, :], z_d[1].rearrange("b p n -> p b n")).then_inc(zg_in, 16)
            for h in range(2, MH):
                head(h)
            sp.wait_ge(pv_done, len(STEPS))
            for b in range(NB):
                sp.dma_start(xs[:, b, :], x_d[b]).then_inc(x_in[b], 16)
            for k in range(RING, KT):
                piece(IN_GROUPS, k, w_out_d[0, k])
            for n in range(1, NH):
                for k in range(KT):
                    piece(IN_GROUPS + n, k, w_out_d[n, k])

            def mlp_pieces(g):
                for k in range(KT):
                    piece(Q_UP + 2 * g, k, w_up_d[g, k])
                for k in range(KT):
                    piece(Q_UP + 1 + 2 * g, k, w_down_d[g, k // NH, k % NH])

            with sp.Fori(0, FG) as g:
                mlp_pieces(g)
            for b in range(NB):
                sp.wait_ge(y_bank_free, 4 + 2 * NB * (FG - 1) + 2 * b + 2)
                sp.dma_start(out_d[b], xs[:, b, :]).then_inc(stored, 16)
            sp.wait_ge(stored, 16 * NB)

        @block.gpsimd
        def _(pool):
            steps = [0]

            def step(ins):
                steps[0] += 1
                ins.then_inc(pool_step, 1)
                pool.wait_ge(pool_step, steps[0])

            def rsqrt(dst, src, n, ready):
                step(pool.tensor_scalar(dst, src, 1.0 / n, EPS, ALU.mult, ALU.add))
                pool.tensor_tensor(dst, dst, minus_half[:, 0:dst.shape[-1]], ALU.pow).then_inc(ready, 1)

            def low_part(q, k):
                pool.wait_ge(whi_done, KT * q + k + 1)
                pool.tensor_tensor(w_lo[:, q % 2, k, :], raw[:, k % RING, :], w_hi[:, q % 2, k, :].bitcast(F32),
                                   ALU.subtract).then_inc(wlo_done, 1)

            def low_part_at(half, count, k):
                pool.wait_ge(whi_done, count + k + 1)
                pool.tensor_tensor(w_lo[:, half, k, :], raw[:, k % RING, :],
                                   w_hi[:, half, k, :].bitcast(F32), ALU.subtract).then_inc(wlo_done, 1)

            def in_low_part(q, k):
                width = ZM if q == 0 else W
                n = KT * q + k
                pool.wait_ge(whi_done, n + 1)
                pool.tensor_tensor(wi_lo[:, n % SLICES, 0:width], raw[:, k % RING, 0:width],
                                   wi_hi[:, n % SLICES, 0:width].bitcast(F32), ALU.subtract).then_inc(wlo_done, 1)

            pool.dma_start(gain[:, :], attn_norm[0].partition_broadcast(P)).then_inc(gain_in, 16)
            pool.dma_start(pos[:, :], positions[0].rearrange("(b p) -> p b", p=P)).then_inc(consts_in, 16)
            pool.dma_start(bg[:, :], b_gate[0].rearrange("(t p) -> p t", p=P)).then_inc(consts_in, 16)
            pool.dma_start(ga[:, 0:2], q_a_norm[0].rearrange("(t p) -> p t", p=P)).then_inc(consts_in, 16)
            pool.dma_start(ga[:, 2:3], kv_a_norm[0].rearrange("(t p) -> p t", p=P)).then_inc(consts_in, 16)
            step(pool.memset(ident[:, :], 0.0))
            pool.affine_select(out=ident[:, :], in_=ident[:, :], compare_op=ALU.not_equal, fill=1.0, base=0,
                               pattern=[[-1, P]], channel_multiplier=1).then_inc(ident_ready, 1)
            step(pool.memset(causal[:, :], 1))
            step(pool.affine_select(out=causal[:, :], in_=causal[:, :], compare_op=ALU.is_ge, fill=0.0,
                                    base=0, pattern=[[1, P]], channel_multiplier=-1))
            pool.memset(minus_half[:, :], -0.5)
            for i in range(HALF):
                last = pool.memset(freq[:, i:i + 1], float(ROPE_BASE ** (-2.0 * i / ROPE)))
            step(last)
            pool.memset(ones[:, :], 1.0).then_inc(ones_ready, 1)

            def x_rstd(b):
                pool.wait_ge(ssq_ready, b + 1)
                rsqrt(rstd[:, 0, b:b + 1], ssq[:, 0, b:b + 1], D, rstd_ready)

            x_rstd(0)
            for k in range(0, 4):
                in_low_part(0, k)
            x_rstd(1)
            for k in range(4, KT):
                in_low_part(0, k)
            for b in range(2, NB):
                x_rstd(b)
            pool.wait_ge(xn_ready, NB)
            pool.dma_start(gqk[:, 0, :], q_head_norm[0].partition_broadcast(P)).then_inc(phase_in, 16)
            pool.dma_start(gqk[:, 1, :], k_head_norm[0].partition_broadcast(P)).then_inc(phase_in, 16)
            pool.dma_start(gn[:, :], gla_out_norm[0].partition_broadcast(P)).then_inc(phase_in, 16)
            pool.dma_start(wgate[:, :], w_gate_up[0]).then_inc(phase_in, 16)
            pool.wait_ge(phase_in, 64)
            pool.tensor_scalar(gqk[:, 0, :], gqk[:, 0, :], SCALE, None, ALU.mult).then_inc(gqk_ready, 1)

            def behind(s):
                b = prep(s, 6)
                if b is not None:
                    pool.wait_ge(c_ss_ready, 2 * b + 2)
                    rsqrt(c_rs[:, b, :], c_ss[:, b, :], 1.0, c_rs_ready)
                b = prep(s, 7)
                if b is not None:
                    if b >= 2:
                        pool.wait_ge(headT_ready, 2 * (b - 1))
                    else:
                        pool.wait_ge(alo_done, 2 * NB)
                    pool.wait_ge(z_out, b + 1)
                    pool.tensor_copy(m_qk[:, b % 2, MH:2 * MH, NOPE:DQK],
                                     zm[:, b, QR + KVR:MLA_W].unsqueeze(1).broadcast_to([P, MH, ROPE])).then_inc(kpe_ready, 1)
                b = prep(s, 9)
                if b is not None:
                    pool.wait_ge(h_ss_ready, b + 1)
                    rsqrt(h_rs[:, :], h_ss[:, :], 1.0, h_rs_ready)

            for q in range(IN_GROUPS):
                for b in range(NB):
                    if q + 1 < IN_GROUPS and b in (0, NB - 1):
                        for k in range(0, 2) if b == 0 else range(2, KT):
                            in_low_part(q + 1, k)
                    behind(NB * q + b)

            pool.wait_ge(z_ready, NB * IN_GROUPS)
            pool.wait_ge(kT_out, NB)
            pool.memset(sc[:, :, :], 0.0).then_inc(sc_zero, 1)
            pool.memset(state[:, :, :, :], 0.0).then_inc(sc_zero, 1)

            def decays(c):
                pool.wait_ge(qkT_out, c + 1)
                pool.wait_ge(g_exp, 4 * c + 3)
                pool.tensor_tensor(g_ke[:, c % 2, :, :], g_ke[:, c % 2, :, :], g_k[:, c % 2, :, :],
                                   ALU.mult).then_inc(ke_ready, 1)
                pool.wait_ge(g_exp, 4 * c + 4)
                pool.tensor_tensor(g_qf[:, c % 2, :, :], g_qf[:, c % 2, :, :], g_q[:, c % 2, :, :],
                                   ALU.mult).then_inc(qf_ready, 1)

            def out_rstd(c):
                pool.wait_ge(g_ss_ready, c + 1)
                rsqrt(g_rs[:, :], g_ss[:, :], GDV, g_rs_ready)

            decays(0)
            for c in range(NB):
                if c >= 1:
                    out_rstd(c - 1)
                if c + 1 < NB:
                    decays(c + 1)
            out_rstd(NB - 1)
            pool.dma_start(gain[:, :], mlp_norm[0].partition_broadcast(P)).then_inc(gain_in, 16)
            for q in range(IN_GROUPS, Q_UP):
                for k in range(KT):
                    low_part(q, k)
            for k in range(KT):
                low_part_at(0, KT * Q_UP, k)
            for b in range(NB):
                pool.wait_ge(ssq_ready, NB + b + 1)
                rsqrt(rstd[:, 1, b:b + 1], ssq[:, 1, b:b + 1], D, rstd_ready)
            for k in range(KT):
                low_part_at(1, KT * (Q_UP + 1), k)
            with pool.Fori(1, FG) as g:
                for half in range(2):
                    for k in range(KT):
                        low_part_at(half, KT * (Q_UP + half) + 2 * KT * g, k)

        @block.scalar
        def _(act):
            steps = [0]

            def step(ins):
                steps[0] += 1
                ins.then_inc(act_step, 1)
                act.wait_ge(act_step, steps[0])

            def copy(dst, src, scale=1.0):
                return act.activation(dst, src, ACT.Copy, scale=scale)

            def in_high_part(q, k):
                width = ZM if q == 0 else W
                n = KT * q + k
                act.wait_ge(raw_in[k % RING], raw_value(q, k))
                if n >= SLICES:
                    q0, k0 = divmod(n - SLICES, KT)
                    if k0 == KT - 1:
                        act.wait_ge(z_ready, NB * (q0 + 1))
                    else:
                        act.wait_ge(slice_free, (KT - 1) * q0 + k0 + 1)
                copy(wi_hi[:, n % SLICES, 0:width], raw[:, k % RING, 0:width]).then_inc(whi_done, 1)

            def high_part(q, k):
                act.wait_ge(raw_in[k % RING], raw_value(q, k))
                copy(w_hi[:, q % 2, k, :], raw[:, k % RING, :]).then_inc(whi_done, 1)

            def high_part_at(half, g, k):
                act.wait_ge(raw_in[k % RING], 16 * (2 * (Q_UP + half) + k // RING + 1) + 32 + 64 * g)
                copy(w_hi[:, half, k, :], raw[:, k % RING, :]).then_inc(whi_done, 1)

            def square_x(r, b):
                if NB * r + b:
                    act.wait_ge(ssq_ready, NB * r + b)
                act.activation(ps[:, 6:8, :].rearrange("p a n -> p (a n)"), (xs if r else x0)[:, b, :], ACT.Square,
                               accum_out=ssq[:, r, b:b + 1]).then_inc(ssq_ready, 1)

            def norm_hi(r, b):
                for j in range(2):
                    n = 2 * (NB * r + b) + j
                    act.wait_ge(xT_ready, n + 1)
                    copy(a_hi[:, 4 * j:4 * j + 4, b * P:(b + 1) * P], bank4(4 + j)).then_inc(ahi_done, 1)

            for b in range(NB):
                act.dma_start(x0[:, b, :], x_d[b]).then_inc(x_in[b], 16)

            def x_square(b):
                act.wait_ge(x_in[b], 16)
                square_x(0, b)

            def behind(s):
                if s == 1:
                    act.wait_ge(rope_arg, 1)
                    act.activation(sin[:, :, :], sin[:, :, :], ACT.Sin).then_inc(rope_ready, 1)
                    act.activation(cos[:, :, :], cos[:, :, :], ACT.Sin).then_inc(rope_ready, 1)
                b = prep(s, 10)
                if b is not None:
                    act.wait_ge(headT_ready, 2 * b + 1)
                    if b >= 1:
                        act.wait_ge(q_stored, 16 * b)
                    copy(q_stage[:, 0:4, :], bank4(4, DQK))
                    copy(q_stage[:, 4:8, :], bank4(5, DQK)).then_inc(qT_out, 1)
                b = prep(s, 6)
                if b is not None:
                    act.wait_ge(z_out, b + 1)
                    for i, (c, n) in enumerate(((0, QR), (QR, KVR))):
                        if b or i:
                            act.wait_ge(c_ss_ready, 2 * b + i)
                        act.activation(junk[:, 0:n], zm[:, b, c:c + n], ACT.Square, scale=float(n) ** -0.5,
                                       accum_out=c_ss[:, b, i:i + 1]).then_inc(c_ss_ready, 1)
                b = prep(s, 7)
                if b is not None:
                    if b == 0:
                        act.wait_ge(alo_done, 2 * NB)
                        act.wait_ge(consts_in, 64)
                    act.wait_ge(cT_ready, b + 1)
                    for i in range(3):
                        last = copy(m_cT[:, i, :], ps[:, 4, i * P:(i + 1) * P], ga[:, i:i + 1])
                    last.then_inc(cT_out, 1)
                if s == 9:
                    act.wait_ge(gateT_ready, 1)
                    for i in range(2):
                        copy(zgateT[:, i * W:(i + 1) * W], ps[0:GR, 5 + i, :]).then_inc(gateT_out, 1)
                b = prep(s, 8)
                if b is not None:
                    qk = m_qk[:, b % 2, :, :]
                    act.wait_ge(qkv_ready, b + 1)
                    if b >= 1:
                        act.wait_ge(v_stored, 16 * b)
                    for i in range(2):
                        copy(qk[:, 4 * i:4 * i + 4, :], ps[:, 4 + i, 0:4 * DQK].rearrange("p (h d) -> p h d", d=DQK))
                    for i in range(2):
                        h = 4 * i
                        kv = bank4(6 + i)
                        copy(qk[:, MH + h:MH + h + 4, 0:NOPE], kv[:, :, 0:NOPE])
                        last = copy(v_stage[:, h * MV:(h + 4) * MV].rearrange("p (h d) -> p h d", d=MV), kv[:, :, NOPE:NOPE + MV])
                    last.then_inc(qkv_out, 1)
                    act.wait_ge(qkv_out, b + 1)
                    act.wait_ge(kpe_ready, b + 1)
                    if b >= 1:
                        act.wait_ge(qk_ready, b)
                    act.activation(m_sq[:, :, :], qk, ACT.Square, scale=float(DQK) ** -0.5).then_inc(sq_ready, 1)
                if s in (13, 16):
                    t = (s - 13) // 3
                    act.wait_ge(logit_out, 2 * t + 2)
                    step(act.activation(g_cum[:, t, :], g_log[:, t, :], ACT.Abs))
                    step(act.activation(g_cum[:, t, :], g_cum[:, t, :], ACT.Exp, scale=-1.0))
                    act.activation(g_cum[:, t, :], g_cum[:, t, :], ACT.Ln, bias=1.0).then_inc(softplus_ready, 1)

            x_square(0)
            for k in range(4):
                in_high_part(0, k)
            x_square(1)
            norm_hi(0, 0)
            for k in range(4, KT):
                in_high_part(0, k)
            for b in range(NB):
                if b + 2 < NB:
                    x_square(b + 2)
                if b + 1 < NB:
                    norm_hi(0, b + 1)
                if b == 1:
                    for k in range(2):
                        in_high_part(1, k)
                if b == NB - 1:
                    for k in range(2, KT):
                        in_high_part(1, k)
                behind(b)
            for q in range(1, IN_GROUPS):
                for b in range(NB):
                    if q == 2:
                        act.wait_ge(z_ready, NB * q + b + 1)
                        if b >= 1:
                            act.wait_ge(z_out, NB * q + b)
                        act.activation(tanh_g[:, :], ps[:, b % 4, :], ACT.Tanh, scale=0.5).then_inc(tanh_ready, 1)
                    if q + 1 < IN_GROUPS and b in (0, NB - 1):
                        for k in range(0, 2) if b == 0 else range(2, KT):
                            in_high_part(q + 1, k)
                    behind(NB * q + b)

            def gla_exps(c):
                act.wait_ge(qkT_ready, c + 1)
                if c >= 2:
                    act.wait_ge(o_ready, c - 1)
                copy(g_q[:, c % 2, :, :], bank4(7)[:, 0:GT, :], float(GDK) ** -0.5)
                copy(g_k[:, c % 2, :, :], bank4(7)[:, GT:2 * GT, :]).then_inc(qkT_out, 1)
                cum = g_cum[:, :, c * P:(c + 1) * P]
                act.wait_ge(from_mid, c + 1)
                act.activation(g_ks[:, c % 2, :, :], g_qs[:, c % 2, :, :], ACT.Exp, scale=-1.0).then_inc(g_exp, 1)
                act.wait_ge(g_exp, 4 * c + 1)
                act.activation(g_qs[:, c % 2, :, :], g_qs[:, c % 2, :, :], ACT.Exp).then_inc(g_exp, 1)
                act.wait_ge(to_last, c + 1)
                act.activation(g_ke[:, c % 2, :, :], g_ke[:, c % 2, :, :], ACT.Exp).then_inc(g_exp, 1)
                act.activation(decay[:, :, c], cum[:, :, P - 1], ACT.Exp)
                act.activation(g_qf[:, c % 2, :, :], cum, ACT.Exp).then_inc(g_exp, 1)

            def gla_mix_hi(c):
                act.wait_ge(ogT_ready, c + 1)
                copy(a_hi[:, 0:GH, c * P:(c + 1) * P], bank4(7)).then_inc(g_mix_hi, 1)

            def gla(c, b):
                if b == 2 and c >= 1:
                    gla_mix_hi(c - 1)
                if b == 4 and c + 1 < NB:
                    act.wait_ge(keT_ready, c + 1)
                    act.wait_ge(sc_ready, 2 * c + 2)
                    copy(ke_tok[:, c, :], ps[:, 7, 2 * P:4 * P]).then_inc(keT_out, 1)
                if b == 6 and c + 1 < NB:
                    gla_exps(c + 1)
                if b == 7:
                    act.wait_ge(o_ready, c + 1)
                    if c >= 1:
                        act.wait_ge(g_ss_ready, c)
                    act.activation(osq[:, :, :], bank4(7), ACT.Square).then_inc(osq_ready, 1)

            def exp(i):
                h, b = STEPS[i]
                nk = (b + 1) * P
                act.wait_ge(max_ready, i + 1)
                if i >= 2:
                    act.wait_ge(pT_ready, 2 * (i - 1))
                act.activation(m_p[:, i % 2, 0:nk], ps[:, 2 * (i % 2):2 * (i % 2) + 2, :].rearrange("p a n -> p (a n)")[:, 0:nk],
                               ACT.Exp, bias=m_nm[:, i % 2:i % 2 + 1],
                               accum_out=m_sum[:, i % 2:i % 2 + 1]).then_inc(p_ready, 1)

            def mla_mix_hi(h, half):
                rows, k, cols = head_out(h, half)
                act.wait_ge(pv_done, NB * h + 4 * half + 4)
                copy(a_hi[rows, k, cols], ps[rows, 6, :]).then_inc(m_mix_hi, 1)

            act.wait_ge(cum_ready, GT)
            act.wait_ge(v_stored, 16 * NB)
            for n in range(2):
                act.wait_ge(z_stored[n], 16 * NB)
            gla_exps(0)
            exp(0)
            for i, (h, b) in enumerate(STEPS):
                if i + 1 < len(STEPS):
                    exp(i + 1)
                act.wait_ge(pT_ready, 2 * i + 1)
                if i >= 2:
                    act.wait_ge(pv_done, i - 1)
                n = min(b + 1, 4)
                copy(m_pT[:, i % 2, 0:n, :], bank4(4)[:, 0:n, :]).then_inc(pT_out, 1)
                if b == 4:
                    mla_mix_hi(h, 0)
                if b == 0 and h >= 1:
                    mla_mix_hi(h - 1, 1)
                gla(h, b)
            mla_mix_hi(MH - 1, 1)
            gla_mix_hi(NB - 1)

            for q in range(IN_GROUPS, Q_UP):
                for k in range(KT):
                    high_part(q, k)
            act.wait_ge(z_ready, NB * (IN_GROUPS + 1))
            for k in range(KT):
                high_part_at(0, 0, k)
            for b in range(NB):
                act.wait_ge(z_out, NB * (Q_UP - 1) + b + 1)
                square_x(1, b)
                if b >= 1:
                    norm_hi(1, b - 1)
            norm_hi(1, NB - 1)
            act.wait_ge(z_ready, NB * Q_UP)
            for k in range(KT):
                high_part_at(1, 0, k)
            act.sem_inc(up_bank_free, 4)

            def group(g, last):
                for j in range(2 * FT):
                    f, half = j // 2, j % 2
                    act.wait_ge(up_ready, 2 * FT * g + j + 1)
                    if j >= 2:
                        act.wait_ge(actlo_done, 2 * FT * g + j - 1)
                    act.activation(relu[:, j % 2, :], ps[:, j % 4, :], ACT.Relu).then_inc(up_bank_free, 1)
                    act.wait_ge(up_bank_free, 4 + 2 * FT * g + j + 1)
                    act.activation(act_hi[:, f, half * W:(half + 1) * W], relu[:, j % 2, :],
                                   ACT.Square).then_inc(acthi_done, 1)
                if not last:
                    for k in range(KT):
                        high_part_at(0, g + 1, k)
                    act.wait_ge(y_ready, 2 * NB * g + 2 * NB)
                    for k in range(KT):
                        high_part_at(1, g + 1, k)

            with act.Fori(0, FG - 1) as g:
                group(g, False)
            group(FG - 1, True)

        @block.vector
        def _(dve):
            steps = [0]

            def step(ins):
                steps[0] += 1
                ins.then_inc(dve_step, 1)
                dve.wait_ge(dve_step, steps[0])

            def stt(out_, in0, scalar, in1, op0, op1):
                return dve.scalar_tensor_tensor(out=out_, in0=in0, scalar=scalar, in1=in1, op0=op0, op1=op1)

            def norm_x(r, b, src, dst):
                dve.wait_ge(rstd_ready, NB * r + b + 1)
                stt(dst, src[:, b, :], rstd[:, r, b:b + 1], gain[:, :], ALU.mult, ALU.mult).then_inc(xn_ready, 1)

            def norm_lo(r, b):
                for j in range(2):
                    n = 2 * (NB * r + b) + j
                    blk = slice(b * P, (b + 1) * P)
                    dve.wait_ge(ahi_done, n + 1)
                    dve.tensor_tensor(a_lo[:, 4 * j:4 * j + 4, blk], bank4(4 + j),
                                      a_hi[:, 4 * j:4 * j + 4, blk].bitcast(F32), ALU.subtract).then_inc(alo_done, 1)

            def rotary_angles():
                dve.wait_ge(consts_in, 64)
                dve.wait_ge(pool_step, POOL_CONSTS)
                step(dve.tensor_copy(rk[:, :, 0], pos[:, :]))
                for i in range(1, HALF):
                    last = dve.tensor_scalar(rk[:, :, i], rk[:, :, 0], freq[:, i:i + 1], None, ALU.mult)
                step(last)
                for table, quarter in ((sin, 0.0), (cos, 0.25)):
                    step(dve.tensor_scalar(table[:, :, :], rk[:, :, :], 1.0 / TWO_PI, quarter, ALU.mult, ALU.add))
                    step(dve.tensor_scalar(table[:, :, :], table[:, :, :], ROUND, -ROUND, ALU.add, ALU.add))
                    step(stt(rt[:, :, :], table[:, :, :], -TWO_PI_A, rk[:, :, :], ALU.mult, ALU.add))
                    step(stt(rt[:, :, :], table[:, :, :], -TWO_PI_B, rt[:, :, :], ALU.mult, ALU.add))
                    step(stt(rt[:, :, :], table[:, :, :], -TWO_PI_C, rt[:, :, :], ALU.mult, ALU.add))
                    step(dve.tensor_scalar(rt[:, :, :], rt[:, :, :], quarter * TWO_PI, PI_SAFE, ALU.add, ALU.min))
                    last = dve.tensor_scalar(table[:, :, :], rt[:, :, :], -PI_SAFE, None, ALU.max)
                    if quarter:
                        last.then_inc(rope_arg, 1)
                    else:
                        step(last)

            def tile_out(s):
                q, b = divmod(s, NB)
                dve.wait_ge(z_ready, s + 1)
                tile = ps[:, s % 4, :]
                n = s - NB
                if 2 <= n < 2 * NB:
                    dve.wait_ge(z_stored[n % 2], 16 * (n // 2))
                if q == 0:
                    dve.tensor_copy(zm[:, b, :], tile[:, 0:ZM]).then_inc(z_out, 1)
                elif q == 1:
                    dve.tensor_copy(z_stage[:, n % 2, :], tile).then_inc(z_out, 1)
                elif q == 2:
                    dve.wait_ge(phase_in, 64)
                    dve.wait_ge(tanh_ready, b + 1)
                    step(stt(z_stage[:, n % 2, :], tanh_g[:, :], 1.0, tile, ALU.add, ALU.mult))
                    g4 = z_stage[:, n % 2, :].rearrange("p (h v) -> p h v", h=GH)
                    stt(g4, g4, 0.5, gn[:, :].unsqueeze(1).broadcast_to([P, GH, GDV]), ALU.mult, ALU.mult).then_inc(z_out, 1)
                else:
                    dve.wait_ge(cum_ready, GT)
                    dve.tensor_copy(zqk[:, b, :], tile).then_inc(z_out, 1)

            def head_norms(b):
                qk = m_qk[:, b % 2, :, :]
                dve.wait_ge(sq_ready, b + 1)
                if b >= 1:
                    dve.wait_ge(h_rs_ready, b)
                dve.tensor_reduce(h_ss[:, :], m_sq[:, :, :], AX.X, ALU.add).then_inc(h_ss_ready, 1)
                dve.wait_ge(h_rs_ready, b + 1)
                step(dve.tensor_tensor(qk, qk, h_rs[:, :].unsqueeze(2).broadcast_to([P, 2 * MH, DQK]), ALU.mult))
                dve.wait_ge(gqk_ready, 1)
                for i in range(2):
                    part = qk[:, i * MH:(i + 1) * MH, :]
                    last = dve.tensor_tensor(part, part, gqk[:, i, :].unsqueeze(1).broadcast_to([P, MH, DQK]), ALU.mult)
                step(last)
                dve.wait_ge(rope_ready, 2)
                pair = qk[:, :, NOPE:DQK].rearrange("p h (a i) -> p h a i", a=2)
                c = cos[:, b, :].unsqueeze(1).unsqueeze(1).broadcast_to([P, 2 * MH, 2, HALF])
                s = sin[:, b, :].unsqueeze(1).unsqueeze(1).broadcast_to([P, 2 * MH, 2, HALF])
                dve.tensor_tensor(m_rc[:, :, :, :], pair, c, ALU.mult)
                step(dve.tensor_tensor(m_rs[:, :, :, :], pair, s, ALU.mult))
                dve.tensor_tensor(pair[:, :, 0, :], m_rc[:, :, 0, :], m_rs[:, :, 1, :], ALU.subtract)
                dve.tensor_tensor(pair[:, :, 1, :], m_rs[:, :, 0, :], m_rc[:, :, 1, :], ALU.add).then_inc(qk_ready, 1)

            def gate_sums(t):
                dve.wait_ge(softplus_ready, t + 1)
                if t == 0:
                    dve.wait_ge(ones_ready, 1)
                step(stt(g_log[:, t, :], g_log[:, t, :], 0.0, g_cum[:, t, :], ALU.min, ALU.subtract))
                step(dve.tensor_scalar(g_log[:, t, :], g_log[:, t, :], 1.0 / GATE_NORM, LOG_GATE_MIN, ALU.mult, ALU.max))
                for b in range(NB):
                    blk = slice(b * P, (b + 1) * P)
                    last = dve.tensor_tensor_scan(g_cum[:, t, blk], ones[:, :], g_log[:, t, blk], 0.0, ALU.mult, ALU.add)
                last.then_inc(cum_ready, 1)

            def behind(s):
                b = prep(s, 10)
                if b is not None:
                    dve.wait_ge(headT_ready, 2 * b + 2)
                    if b >= 1:
                        dve.wait_ge(k_stored, 16 * b)
                    dve.tensor_copy(k_stage[:, 0:4, :], bank4(6, DQK))
                    dve.tensor_copy(k_stage[:, 4:8, :], bank4(7, DQK)).then_inc(kT_out, 1)
                b = prep(s, 6)
                if b is not None:
                    dve.wait_ge(c_rs_ready, b + 1)
                    dve.tensor_scalar(zm[:, b, 0:QR], zm[:, b, 0:QR], c_rs[:, b, 0:1], None, ALU.mult)
                    dve.tensor_scalar(zm[:, b, QR:QR + KVR], zm[:, b, QR:QR + KVR], c_rs[:, b, 1:2], None,
                                      ALU.mult).then_inc(c_ready, 1)
                if s in (12, 15):
                    t = (s - 12) // 3
                    for i in range(2):
                        dve.wait_ge(logit_ready, 2 * t + i + 1)
                        dve.tensor_scalar(g_log[:, t, i * W:(i + 1) * W], ps[:, 5 + i, :], bg[:, t:t + 1], None,
                                          ALU.add).then_inc(logit_out, 1)
                if s in (14, 17):
                    gate_sums((s - 14) // 3)
                b = prep(s, 9)
                if b is not None:
                    head_norms(b)

            dve.wait_ge(gain_in, 16)
            norm_x(0, 0, x0, x0[:, 0, :])
            norm_x(0, 1, x0, x0[:, 1, :])
            norm_lo(0, 0)
            for b in range(NB):
                if b + 2 < NB:
                    norm_x(0, b + 2, x0, x0[:, b + 2, :])
                if b + 1 < NB:
                    norm_lo(0, b + 1)
                if b == 1:
                    rotary_angles()
                tile_out(b)
                behind(b)
            for s in range(NB, NB * IN_GROUPS):
                tile_out(s)
                behind(s)

            def gla_decays(c):
                cum = g_cum[:, :, c * P:(c + 1) * P]
                if c >= 2:
                    dve.wait_ge(o_ready, c - 1)
                dve.tensor_tensor(g_qs[:, c % 2, :, :], cum, cum[:, :, CHUNK - 1:CHUNK].broadcast_to([P, GT, P]),
                                  ALU.subtract).then_inc(from_mid, 1)
                dve.tensor_tensor(g_ke[:, c % 2, :, :], cum[:, :, P - 1:P].broadcast_to([P, GT, P]), cum,
                                  ALU.subtract).then_inc(to_last, 1)

            def gla_decayed(c):
                dve.wait_ge(qkT_out, c + 1)
                dve.wait_ge(g_exp, 4 * c + 2)
                dve.tensor_tensor(g_qs[:, c % 2, :, :], g_qs[:, c % 2, :, :], g_q[:, c % 2, :, :], ALU.mult).then_inc(qs_ready, 1)
                dve.tensor_tensor(g_ks[:, c % 2, :, :], g_ks[:, c % 2, :, :], g_k[:, c % 2, :, :], ALU.mult).then_inc(qs_ready, 1)

            def gla_mask(c, odd):
                dve.wait_ge(scT_ready, 2 * c + odd + 1)
                if c >= 1:
                    dve.wait_ge(o_ready, c)
                else:
                    dve.wait_ge(sc_zero, 2)
                dve.copy_predicated(sc[:, odd::2, :], causal[:, :].unsqueeze(1).broadcast_to([P, GT, P]),
                                    bank4(7)[:, 0:GT, :]).then_inc(sc_ready, 1)

            def gla_state(c):
                dve.wait_ge(kv_ready, c + 1)
                dve.wait_ge(g_exp, 4 * c + 4)
                if c >= 1:
                    dve.wait_ge(o_ready, c)
                    dve.wait_ge(state_ready, c)
                for t in range(GT):
                    for s in range(2):
                        rows = slice(s * GDK, (s + 1) * GDK)
                        kv = ps[rows, 7, (2 * t + s) * GDV:(2 * t + s + 1) * GDV]
                        own = slice(s * GDV, (s + 1) * GDV)
                        last = stt(state[rows, (c + 1) % 2, t, own], state[rows, c % 2, t, own],
                                   decay[rows, t, c:c + 1], kv, ALU.mult, ALU.add)
                last.then_inc(state_ready, 1)

            def gla_sums(c):
                dve.wait_ge(osq_ready, c + 1)
                if c >= 1:
                    dve.wait_ge(g_rs_ready, c)
                dve.tensor_reduce(g_ss[:, :], osq[:, :, :], AX.X, ALU.add).then_inc(g_ss_ready, 1)

            def gla_out(c):
                dve.wait_ge(g_rs_ready, c + 1)
                if c >= 1:
                    dve.wait_ge(ogT_ready, c)
                else:
                    dve.wait_ge(zg_in, 16)
                step(dve.tensor_tensor(og[:, :, :], bank4(7), g_rs[:, :].unsqueeze(2).broadcast_to([P, GH, GDV]), ALU.mult))
                g4 = zg[:, c, :].rearrange("p (h v) -> p h v", h=GH)
                dve.tensor_tensor(og[:, :, :], og[:, :, :], g4, ALU.mult).then_inc(og_ready, 1)

            def gla_lo(c):
                blk = slice(c * P, (c + 1) * P)
                dve.wait_ge(g_mix_hi, c + 1)
                dve.tensor_tensor(a_lo[:, 0:GH, blk], bank4(7), a_hi[:, 0:GH, blk].bitcast(F32),
                                  ALU.subtract).then_inc(g_mix_lo, 1)

            def gla(c, b):
                if c >= 1 and b <= 2:
                    (gla_sums, gla_out, gla_lo)[b](c - 1)
                if b in (3, 4):
                    gla_mask(c, b - 3)
                if c + 1 < NB:
                    if b == 5:
                        gla_state(c)
                    if b == 6:
                        gla_decays(c + 1)
                    if b == 7:
                        gla_decayed(c + 1)

            def row_max(i):
                h, b = STEPS[i]
                nk = (b + 1) * P
                s = ps[:, 2 * (i % 2):2 * (i % 2) + 2, :].rearrange("p a n -> p (a n)")
                dve.wait_ge(s_ready, i + 1)
                step(dve.memset(s[0:CHUNK, nk - CHUNK:nk], MASKED))
                if i >= 2:
                    dve.wait_ge(p_ready, i - 1)
                dve.tensor_reduce(m_nm[:, i % 2:i % 2 + 1], s[:, 0:nk], AX.X, ALU.max, negate=True).then_inc(max_ready, 1)

            def normalise(i):
                h, b = STEPS[i]
                nk = (b + 1) * P
                dve.wait_ge(p_ready, i + 1)
                step(dve.reciprocal(m_rden[:, i % 2:i % 2 + 1], m_sum[:, i % 2:i % 2 + 1]))
                dve.tensor_scalar(m_p[:, i % 2, 0:nk], m_p[:, i % 2, 0:nk], m_rden[:, i % 2:i % 2 + 1], None,
                                  ALU.mult).then_inc(pn_ready, 1)

            def mla_mix_lo(h, half):
                rows, k, cols = head_out(h, half)
                dve.wait_ge(m_mix_hi, 2 * h + half + 1)
                dve.tensor_tensor(a_lo[rows, k, cols], ps[rows, 6, :], a_hi[rows, k, cols].bitcast(F32),
                                  ALU.subtract).then_inc(m_mix_lo, 1)

            dve.wait_ge(z_stored[1], 16 * NB)
            gla_decays(0)
            gla_decayed(0)
            row_max(0)
            row_max(1)
            normalise(0)
            for i, (h, b) in enumerate(STEPS):
                if i + 2 < len(STEPS):
                    row_max(i + 2)
                if i + 1 < len(STEPS):
                    normalise(i + 1)
                if b >= SECOND:
                    dve.wait_ge(pT_ready, 2 * i + 2)
                    if i >= 2:
                        dve.wait_ge(pv_done, i - 1)
                    dve.tensor_copy(m_pT[:, i % 2, 4:b + 1, :], bank4(5)[:, 0:b - 3, :]).then_inc(pT_out2, 1)
                if b == SECOND:
                    mla_mix_lo(h, 0)
                if b == 0 and h >= 1:
                    mla_mix_lo(h - 1, 1)
                gla(h, b)
            mla_mix_lo(MH - 1, 1)
            gla_sums(NB - 1)
            gla_out(NB - 1)
            gla_lo(NB - 1)

            def residual(n, b):
                m = NB * (IN_GROUPS + n) + b
                dve.wait_ge(z_ready, m + 1)
                if n == 0:
                    dve.wait_ge(x_in[b], 32)
                xh = xs[:, b, n * W:(n + 1) * W]
                dve.tensor_tensor(xh, ps[:, m % 4, :], xh, ALU.add).then_inc(z_out, 1)

            for b in range(NB):
                residual(0, b)
            dve.wait_ge(gain_in, 32)
            for b in range(NB):
                residual(1, b)
                if b >= 1:
                    if b - 1 >= 2:
                        dve.wait_ge(xT_ready, 2 * (NB + b - 2))
                    norm_x(1, b - 1, xs, xn2[:, (b - 1) % 2, :])
                if b >= 2:
                    norm_lo(1, b - 2)
            dve.wait_ge(xT_ready, 2 * (NB + NB - 2))
            norm_x(1, NB - 1, xs, xn2[:, (NB - 1) % 2, :])
            norm_lo(1, NB - 2)
            norm_lo(1, NB - 1)
            dve.sem_inc(y_bank_free, 4)

            def group(g):
                for j in range(2 * FT):
                    f, half = j // 2, j % 2
                    cols = slice(half * W, (half + 1) * W)
                    dve.wait_ge(acthi_done, 2 * FT * g + j + 1)
                    dve.tensor_tensor(relu[:, j % 2, :], relu[:, j % 2, :], relu[:, j % 2, :],
                                      ALU.mult).then_inc(relu_ready, 1)
                    dve.wait_ge(relu_ready, 2 * FT * g + j + 1)
                    dve.tensor_tensor(act_lo[:, f, cols], relu[:, j % 2, :], act_hi[:, f, cols].bitcast(F32),
                                      ALU.subtract).then_inc(actlo_done, 1)
                for t in range(2 * NB):
                    b, n = t // 2, t % 2
                    dve.wait_ge(y_ready, 2 * NB * g + t + 1)
                    xh = xs[:, b, n * W:(n + 1) * W]
                    dve.tensor_tensor(xh, ps[:, 4 + t % 4, :], xh, ALU.add).then_inc(y_bank_free, 1)

            with dve.Fori(0, FG) as g:
                group(g)

        @block.tensor
        def _(pe):
            def mm(dst, lhsT, rhs, start, stop):
                return pe.matmul(dst, lhsT, rhs, start=start, stop=stop)

            def split_product(dst, hi, lo, rhs_hi, rhs_lo, first, last):
                mm(dst, hi, rhs_hi, first, False)
                mm(dst, hi, rhs_lo, False, False)
                return mm(dst, lo, rhs_hi, False, last)

            def norm_T(r, b, src):
                pe.wait_ge(xn_ready, NB * r + b + 1)
                for j in range(2):
                    n = 2 * (NB * r + b) + j
                    if n >= 2:
                        pe.wait_ge(alo_done, n - 1)
                    for i in range(4):
                        last = pe.transpose(bank4(4 + j)[:, i, :], src[:, (4 * j + i) * P:(4 * j + i + 1) * P], ident[:, :])
                    last.then_inc(xT_ready, 1)

            def in_project(q, b):
                n = NB * q + b
                blk = slice(b * P, (b + 1) * P)
                width = ZM if q == 0 else W
                if n >= 4:
                    pe.wait_ge(z_out, n - 3)
                for k in range(KT):
                    if b == 0:
                        pe.wait_ge(wlo_done, KT * q + k + 1)
                    w = (KT * q + k) % SLICES
                    last = split_product(ps[:, n % 4, 0:width], a_hi[:, k, blk], a_lo[:, k, blk],
                                         wi_hi[:, w, 0:width], wi_lo[:, w, 0:width], k == 0, k == KT - 1)
                    if b == NB - 1 and k < KT - 1:
                        last.then_inc(slice_free, 1)
                last.then_inc(z_ready, 1)

            def project(q, b):
                n = NB * q + b
                blk = slice(b * P, (b + 1) * P)
                pe.wait_ge(z_out, n - 3)
                for k in range(KT):
                    if b == 0:
                        pe.wait_ge(wlo_done, KT * q + k + 1)
                    last = split_product(ps[:, n % 4, :], a_hi[:, k, blk], a_lo[:, k, blk],
                                         w_hi[:, q % 2, k, :], w_lo[:, q % 2, k, :], k == 0, k == KT - 1)
                last.then_inc(z_ready, 1)

            def behind(s):
                b = prep(s, 10)
                if b is not None:
                    pe.wait_ge(qk_ready, b + 1)
                    pe.wait_ge(gateT_out, 2)
                    if s >= 12:
                        pe.wait_ge(logit_out, 2 if s < 15 else 4)
                    for i in range(2 * MH):
                        last = pe.transpose(bank4(4 + i // 4, DQK)[:, i % 4, :], m_qk[:, b % 2, i, :], ident[:, :])
                        if i % MH == MH - 1:
                            last.then_inc(headT_ready, 1)
                b = prep(s, 7)
                if b is not None:
                    pe.wait_ge(c_ready, b + 1)
                    if b == 0:
                        pe.wait_ge(alo_done, 2 * NB)
                    else:
                        pe.wait_ge(qkv_out, b)
                        pe.wait_ge(qT_out, b)
                    for i in range(3):
                        last = pe.transpose(ps[:, 4, i * P:(i + 1) * P], zm[:, b, i * P:(i + 1) * P], ident[:, :])
                    last.then_inc(cT_ready, 1)
                b = prep(s, 8)
                if b is not None:
                    if b == 0:
                        pe.wait_ge(mla_w_in, 32)
                        pe.wait_ge(ssq_ready, NB)
                    else:
                        pe.wait_ge(kT_out, b)
                    pe.wait_ge(cT_out, b + 1)
                    for j in range(2):
                        for i in range(QR // P):
                            mm(ps[:, 4 + j, 0:4 * DQK], m_cT[:, i, :], m_uq[:, i, 4 * j * DQK:4 * (j + 1) * DQK],
                               i == 0, i == QR // P - 1)
                    for j in range(2):
                        last = mm(ps[:, 6 + j, :], m_cT[:, 2, :], m_ukv[:, j * W:(j + 1) * W], True, True)
                    last.then_inc(qkv_ready, 1)
                if s == 9:
                    pe.wait_ge(z_out, NB)
                    pe.wait_ge(qkv_out, 1)
                    for b in range(NB):
                        last = pe.transpose(bank4(5 + b // 4, GR)[:, b % 4, :], zm[:, b, MLA_W:ZM], ident[:, :])
                    last.then_inc(gateT_ready, 1)
                if s in (12, 15):
                    t = (s - 12) // 3
                    pe.wait_ge(qkv_out, t + 2)
                    pe.wait_ge(qT_out, t + 1)
                    pe.wait_ge(kT_out, t + 1)
                    pe.wait_ge(phase_in, 64)
                    for i in range(2):
                        mm(ps[:, 5 + i, :], wgate[:, t * P:(t + 1) * P], zgateT[:, i * W:(i + 1) * W],
                           True, True).then_inc(logit_ready, 1)

            pe.wait_ge(ident_ready, 1)
            norm_T(0, 0, x0[:, 0, :])
            for b in range(NB):
                if b + 1 < NB:
                    norm_T(0, b + 1, x0[:, b + 1, :])
                pe.wait_ge(alo_done, 2 * b + 2)
                in_project(0, b)
                behind(b)
            for q in range(1, IN_GROUPS):
                for b in range(NB):
                    in_project(q, b)
                    behind(NB * q + b)

            def gla_qkT(c):
                if c >= 1:
                    pe.wait_ge(state_ready, c)
                for i in range(2 * GT):
                    last = pe.transpose(bank4(7)[:, i, :], zqk[:, c, i * P:(i + 1) * P], ident[:, :])
                last.then_inc(qkT_ready, 1)

            def gla_scores(c, odd):
                rows = slice(odd * GDK, (odd + 1) * GDK)
                for t in range(GT):
                    last = mm(bank4(7)[:, t, :], g_ks[rows, c % 2, t, :], g_qs[rows, c % 2, t, :], True, True)
                last.then_inc(scT_ready, 1)

            def gla(c, b):
                if b == 2 and c >= 1:
                    pe.wait_ge(og_ready, c)
                    for h in range(GH):
                        last = pe.transpose(bank4(7)[:, h, :], og[:, h, :], ident[:, :])
                    last.then_inc(ogT_ready, 1)
                if b == 3:
                    pe.wait_ge(qs_ready, 2 * c + 2)
                    if c >= 1:
                        pe.wait_ge(g_mix_lo, c)
                    gla_scores(c, 0)
                if b == 4:
                    pe.wait_ge(sc_ready, 2 * c + 1)
                    if c + 1 < NB:
                        pe.wait_ge(ke_ready, c + 1)
                        for t in range(GT):
                            last = pe.transpose(bank4(7)[:, GT + t, :], g_ke[:, c % 2, t, :], ident[:, :])
                        last.then_inc(keT_ready, 1)
                    gla_scores(c, 1)
                if b == 5 and c + 1 < NB:
                    pe.wait_ge(keT_out, c + 1)
                    if c == 0:
                        pe.wait_ge(zv_in, 16)
                    for t in range(GT):
                        last = mm(ps[:, 7, 2 * t * GDV:2 * (t + 1) * GDV], ke_tok[:, c, t * P:(t + 1) * P],
                                  zv[:, c, 2 * t * GDV:2 * (t + 1) * GDV], True, True)
                    last.then_inc(kv_ready, 1)
                if b == 6 and c + 1 < NB:
                    gla_qkT(c + 1)
                if b == 7:
                    pe.wait_ge(qf_ready, c + 1)
                    if c + 1 < NB:
                        pe.wait_ge(qkT_out, c + 2)
                    else:
                        pe.wait_ge(sc_ready, 2 * NB)
                    for t in range(GT):
                        mm(ps[:, 7, 2 * t * GDV:2 * (t + 1) * GDV], g_qf[:, c % 2, t, :], state[:, c % 2, t, :],
                           True, False)
                        for h in (2 * t, 2 * t + 1):
                            last = mm(bank4(7)[:, h, :], sc[:, h, :], zv[:, c, h * GDV:(h + 1) * GDV],
                                      False, h % 2 == 1)
                    last.then_inc(o_ready, 1)

            def scores(i):
                h, b = STEPS[i]
                nk = (b + 1) * P
                if i >= 2:
                    pe.wait_ge(p_ready, i - 1)
                if b == 0:
                    pe.wait_ge(head_in[h % 2], 32 * (h // 2 + 1))
                for c in range(0, nk, W):
                    n = min(W, nk - c)
                    last = mm(ps[:, 2 * (i % 2) + c // W, 0:n], m_qT[:, h % 2, b * P:(b + 1) * P],
                              m_kT[:, h % 2, c:c + n], True, True)
                last.then_inc(s_ready, 1)

            def p_transposes(i):
                h, b = STEPS[i]
                pe.wait_ge(pn_ready, i + 1)
                if i >= 1:
                    pe.wait_ge(pT_out, i)
                if seconds(i):
                    pe.wait_ge(pT_out2, seconds(i))
                for c in range(b + 1):
                    last = pe.transpose(bank4(4 + c // 4)[:, c % 4, :], m_p[:, i % 2, c * P:(c + 1) * P], ident[:, :])
                    if c == min(b, 3):
                        last.then_inc(pT_ready, 1 if b >= SECOND else 2)
                if b >= SECOND:
                    last.then_inc(pT_ready, 1)

            def values(i):
                h, b = STEPS[i]
                pe.wait_ge(pT_out, i + 1)
                if b >= SECOND:
                    pe.wait_ge(pT_out2, seconds(i) + 1)
                if i == 0:
                    pe.wait_ge(v_in[0], 16)
                if b == SECOND:
                    pe.wait_ge(v_in[1], 16)
                    pe.wait_ge(m_mix_lo, 2 * h + 1)
                if b == 0 and h >= 1:
                    pe.wait_ge(m_mix_lo, 2 * h)
                rows, _, _ = head_out(h, 0)
                dst = ps[rows, 6, (b % 4) * P:(b % 4 + 1) * P]
                for c in range(b + 1):
                    last = mm(dst, m_v[:, c, h * MV:(h + 1) * MV], m_pT[:, i % 2, c, :], c == 0, c == b)
                last.then_inc(pv_done, 1)

            pe.wait_ge(z_out, NB * IN_GROUPS)
            pe.wait_ge(qT_out, NB)
            pe.wait_ge(kT_out, NB)
            gla_qkT(0)
            scores(0)
            scores(1)
            for i, (h, b) in enumerate(STEPS):
                if i + 2 < len(STEPS):
                    scores(i + 2)
                p_transposes(i)
                if i >= 1:
                    values(i - 1)
                gla(h, b)
            values(len(STEPS) - 1)
            gla(NB, 2)

            for n in range(NH):
                for b in range(NB):
                    if n == 0:
                        pe.wait_ge(m_mix_lo, 2 * MH - 1 if b < SECOND else 2 * MH)
                        pe.wait_ge(g_mix_lo, NB)
                    project(IN_GROUPS + n, b)
                    if n == NH - 1 and b >= 2:
                        norm_T(1, b - 2, xn2[:, b % 2, :])
            norm_T(1, NB - 2, xn2[:, NB % 2, :])
            norm_T(1, NB - 1, xn2[:, (NB - 1) % 2, :])

            def group(g, first):
                for j in range(2 * FT):
                    f, half = j // 2, j % 2
                    cols = slice(half * W, (half + 1) * W)
                    pe.wait_ge(up_bank_free, 2 * FT * g + j + 1)
                    for k in range(KT):
                        if j == 0:
                            pe.wait_ge(wlo_done, 2 * KT * g + KT * Q_UP + k + 1)
                        wh = w_hi[:, 0, k, f * P:(f + 1) * P]
                        wl = w_lo[:, 0, k, f * P:(f + 1) * P]
                        last = split_product(ps[:, j % 4, :], wh, wl, a_hi[:, k, cols], a_lo[:, k, cols],
                                             k == 0, k == KT - 1)
                    last.then_inc(up_ready, 1)
                for quad in range(NB // 2):
                    for f in range(FT):
                        pe.wait_ge(actlo_done, 2 * FT * g + 2 * f + quad // 2 + 1)
                        for s in range(4):
                            t = 4 * quad + s
                            b, n = t // 2, t % 2
                            blk = slice(b * P, (b + 1) * P)
                            if f == 0:
                                pe.wait_ge(y_bank_free, 2 * NB * g + t + 1)
                            if quad == 0 and s < 2:
                                pe.wait_ge(wlo_done, 2 * KT * g + KT * (Q_UP + 1) + 2 * f + n + 1)
                            kk = 2 * f + n
                            last = split_product(ps[:, 4 + s, :], act_hi[:, f, blk], act_lo[:, f, blk],
                                                 w_hi[:, 1, kk, :], w_lo[:, 1, kk, :], f == 0, f == FT - 1)
                            if f == FT - 1:
                                last.then_inc(y_ready, 1)

            pe.wait_ge(alo_done, 4 * NB)
            with pe.Fori(0, FG) as g:
                group(g, False)


_INS = ['x', 'positions', 'attn_norm', 'w_in', 'w_gate_up', 'b_gate', 'gla_out_norm', 'q_a_norm', 'w_uq',
        'kv_a_norm', 'w_ukv', 'q_head_norm', 'k_head_norm', 'w_out', 'mlp_norm', 'w_up', 'w_down']


def kernel(**inputs):
    import numpy as _np
    import concourse.bacc as _bacc
    from concourse import mybir as _mybir
    from concourse.bass_utils import run_bass_kernel_spmd as _run

    nc = _bacc.Bacc("TRN2", target_bir_lowering=False, num_devices=1)
    arrays, args = {}, []
    for name in _INS:
        a = _np.ascontiguousarray(inputs[name])
        arrays[f"in_{name}_dram"] = a
        args.append(nc.dram_tensor(f"in_{name}_dram", a.shape, _mybir.dt.from_np(a.dtype), kind="ExternalInput").ap())
    out = nc.dram_tensor("out_0_dram", (1, T, D), F32, kind="ExternalOutput").ap()
    layer(nc, *args, out)
    r = _run(nc, [arrays], core_ids=[0])
    return r.results[0]["out_0_dram"]
```

```python
from contextlib import ExitStack

import concourse.bass as bass
from concourse import mybir

F32 = mybir.dt.float32
F32R = mybir.dt.float32r
I32 = mybir.dt.int32
ALU = mybir.AluOpType
ACT = mybir.ActivationFunctionType
AX = mybir.AxisListType

P = 128
T, D, FF = 1024, 1024, 4096
NB = T // P
KT = D // P
W = 512
NH = D // W
EPS = 1e-6

CHUNK = 64
GH, GDK, GDV, GR = 4, 64, 128, 16
GT = GH * GDK // P
GATE_NORM, LOG_GATE_MIN = 16.0, -1.0

MH, QR, KVR, NOPE, ROPE, MV = 8, 256, 128, 64, 32, 64
DQK = NOPE + ROPE
HALF = ROPE // 2
ROPE_BASE = 10000.0
SCALE = float(DQK) ** -0.5
MASKED = -1e30

C_QK, C_V, C_GATE, C_G, C_MLA = 0, 512, 1024, 1040, 1552
MLA_W = QR + KVR + ROPE
ZM = MLA_W + GR

RING = 4
SLICES = 10
FG = FF // W
FT = W // P
IN_GROUPS, OUT_GROUPS = 4, NH

TWO_PI = 6.283185307179586
TWO_PI_A = 6.28125
TWO_PI_B = 0.0019350051879882812
TWO_PI_C = TWO_PI - TWO_PI_A - TWO_PI_B
ROUND = 12582912.0
PI_SAFE = 3.1415925


def layer(nc, x, positions, attn_norm, w_in, w_gate_up, b_gate, gla_out_norm, q_a_norm, w_uq,
          kv_a_norm, w_ukv, q_head_norm, k_head_norm, w_out, mlp_norm, w_up, w_down, out):
    x_d = x[0].rearrange("(b p) d -> b p d", p=P)
    out_d = out[0].rearrange("(b p) d -> b p d", p=P)
    w_in_d = w_in[0].rearrange("(k p) n -> k p n", p=P)
    w_out_d = w_out[0].rearrange("(k p) (h n) -> h k p n", p=P, n=W)
    w_up_d = w_up[0].rearrange("(k p) (g n) -> g k p n", p=P, n=W)
    w_down_d = w_down[0].rearrange("(g f p) (h n) -> g f h p n", p=P, f=FT, n=W)

    ctx = ExitStack()
    with ctx:
        ctx.enter_context(nc.allow_non_contiguous_dma(reason="gains and positions of a few KB, laid by partition"))

        def sem(name):
            return ctx.enter_context(nc.semaphore(name))

        base = -(-nc.sbuf_base // 64) * 64
        KB = 1024

        def at(name, shape, offset, dt=F32):
            return nc.alloc_sbuf_tensor_at(name, shape, dt, offset=base + offset)

        A, B, X, E, RAW, GB, C = 0, 64 * KB, 128 * KB, 160 * KB, 192 * KB, 200 * KB, 204 * KB
        a_hi = at("a_hi", [P, KT, T], A, F32R)
        a_lo = at("a_lo", [P, KT, T], A + 32 * KB, F32R)
        raw = at("raw", [P, RING, W], RAW)

        x0 = at("x0", [P, NB, D], X)
        gain = at("gain", [P, D], GB)
        wi_hi = at("wi_hi", [P, SLICES, W], B, F32R)
        wi_lo = at("wi_lo", [P, SLICES, W], B + 20 * KB, F32R)
        zqk = at("zqk", [P, NB, W], 104 * KB)
        g_cum = at("g_cum", [P, GT, T], 120 * KB)
        g_log = at("g_log", [P, GT, T], 104 * KB)
        zgateT = at("zgateT", [GR, T], 112 * KB)
        ones = at("ones", [P, P], 116 * KB)
        rk = at("rk", [P, NB, HALF], 117 * KB)
        rt = at("rt", [P, NB, HALF], 117 * KB + 512)
        freq = at("freq", [P, HALF], 118 * KB)
        m_qk = at("m_qk", [P, 2, 2 * MH, DQK], 128 * KB)
        m_sq = at("m_sq", [P, 2 * MH, DQK], 140 * KB)
        m_rc = at("m_rc", [P, 2 * MH, 2, HALF], 158 * KB)
        m_rs = at("m_rs", [P, 2 * MH, 2, HALF], 190 * KB)
        m_uq = at("m_uq", [P, QR // P, MH * DQK], 146 * KB)
        m_ukv = at("m_ukv", [P, MH * (NOPE + MV)], 152 * KB)
        m_cT = at("m_cT", [P, 3, P], 156 * KB)
        q_stage = at("q_stage", [DQK, MH, P], 160 * KB)
        k_stage = at("k_stage", [DQK, MH, P], 164 * KB)
        v_stage = at("v_stage", [P, MH * MV], 168 * KB)
        z_stage = at("z_stage", [P, 2, W], 170 * KB)
        zm = at("zm", [P, NB, ZM], 174 * KB)
        tanh_g = at("tanh_g", [P, W], 188 * KB)
        junk = at("junk", [P, QR], 118 * KB + 512)
        gqk = at("gqk", [P, 2, DQK], GB)
        gn = at("gn", [P, GDV], GB + 768)
        wgate = at("wgate", [GR, GH * GDK], GB + 1280)

        zv = at("zv", [P, NB, W], 72 * KB)
        zg = at("zg", [P, NB, W], 88 * KB)
        m_p = at("m_p", [P, 2, T], B)
        m_v = at("m_v", [P, NB, MH * MV], 128 * KB)
        m_qT = at("m_qT", [DQK, 2, T], 144 * KB)
        m_kT = at("m_kT", [DQK, 2, T], 152 * KB)
        m_pT = at("m_pT", [P, 2, NB, P], 160 * KB)
        g_q, g_k, g_qs, g_ks, g_ke, g_qf = (at(f"g_{name}", [P, 2, GT, P], 168 * KB + 2 * KB * n)
                                            for n, name in enumerate(("q", "k", "qs", "ks", "ke", "qf")))
        sc = at("sc", [P, GH, P], 180 * KB)
        state = at("state", [P, 2, GT, 2 * GDV], 182 * KB)
        og = at("og", [P, GH, GDV], 186 * KB)
        osq = at("osq", [P, GH, GDV], 188 * KB)
        om = at("om", [P, NB, 2 * MV], GB)
        ke_tok = zqk[:, :, 0:GH * GDK]

        w_hi = [at(f"w_hi{half}", [P, KT, W], 96 * KB - 32 * KB * half, F32R) for half in range(2)]
        w_lo = [at(f"w_lo{half}", [P, KT, W], 112 * KB - 32 * KB * half, F32R) for half in range(2)]
        xs = at("xs", [P, NB, D], X)
        act_hi = at("act_hi", [P, FT, T], E, F32R)
        act_lo = at("act_lo", [P, FT, T], E + 16 * KB, F32R)
        xn2 = at("xn2", [P, 2, D], E + 24 * KB)
        relu = at("relu", [P, 2, W], GB)

        q_d = nc.dram_tensor("q_heads", (MH, DQK, T), F32, kind="Internal").ap()
        k_d = nc.dram_tensor("k_heads", (MH, DQK, T), F32, kind="Internal").ap()
        v_d = nc.dram_tensor("v_heads", (NB, P, MH * MV), F32, kind="Internal").ap()
        z_d = nc.dram_tensor("z_gla", (2, NB, P, W), F32, kind="Internal").ap()

        place = [C]

        def small(name, shape, dt=F32):
            size = 4
            for n in shape[1:]:
                size *= n
            t = at(name, shape, place[0], dt)
            place[0] += -(-size // 32) * 32
            return t

        ident = small("ident", [P, P])
        causal = small("causal", [P, P], I32)
        cos = small("cos", [P, NB, HALF])
        sin = small("sin", [P, NB, HALF])
        pos = small("pos", [P, NB], I32)
        minus_half = small("minus_half", [P, 2 * MH])
        bg = small("bg", [P, GT])
        ga = small("ga", [P, 3])
        ssq = small("ssq", [P, 2, NB])
        rstd = small("rstd", [P, 2, NB])
        decay = small("decay", [P, GT, NB])
        g_ss = small("g_ss", [P, GH])
        g_rs = small("g_rs", [P, GH])
        c_ss = small("c_ss", [P, NB, 2])
        c_rs = small("c_rs", [P, NB, 2])
        h_ss = small("h_ss", [P, 2 * MH])
        h_rs = small("h_rs", [P, 2 * MH])
        m_nm = small("m_nm", [P, 2])
        m_sum = small("m_sum", [P, 2, NB])
        m_rden = small("m_rden", [P, NB])
        assert base + place[0] <= nc.sbuf_usable_end

        ps = ctx.enter_context(nc.psum_tensor("ps", [P, 8, W], F32))

        def bank4(n, parts=P):
            return ps[0:parts, n, :].rearrange("p (h c) -> p h c", c=P)

        x_in = [sem(f"x_in{b}") for b in range(NB)]
        raw_in = [sem(f"raw_in{s}") for s in range(RING)]
        gain_in, consts_in, phase_in, mla_w_in = sem("gain_in"), sem("consts_in"), sem("phase_in"), sem("mla_w_in")
        stored = sem("stored")
        ident_ready, pool_step, dve_step, act_step = sem("ident_ready"), sem("pool_step"), sem("dve_step"), sem("act_step")
        whi_done, wlo_done = sem("whi_done"), sem("wlo_done")
        ssq_ready, rstd_ready, xn_ready = sem("ssq_ready"), sem("rstd_ready"), sem("xn_ready")
        xT_ready, ahi_done, alo_done = sem("xT_ready"), sem("ahi_done"), sem("alo_done")
        z_ready, z_out = sem("z_ready"), sem("z_out")
        gqk_ready = sem("gqk_ready")
        rope_arg, rope_ready = sem("rope_arg"), sem("rope_ready")
        slice_free = sem("slice_free")
        qkT_ready, qkT_out, gateT_ready, gateT_out = sem("qkT_ready"), sem("qkT_out"), sem("gateT_ready"), sem("gateT_out")
        logit_ready, logit_out, softplus_ready = sem("logit_ready"), sem("logit_out"), sem("softplus_ready")
        from_mid, to_last, g_exp = sem("from_mid"), sem("to_last"), sem("g_exp")
        qs_ready, ke_ready, keT_ready, keT_out = sem("qs_ready"), sem("ke_ready"), sem("keT_ready"), sem("keT_out")
        tanh_ready, ones_ready = sem("tanh_ready"), sem("ones_ready")
        scT_ready, sc_ready, sc_zero, kv_ready, state_ready = sem("scT_ready"), sem("sc_ready"), sem("sc_zero"), sem("kv_ready"), sem("state_ready")
        o_ready, osq_ready, g_ss_ready, g_rs_ready, og_ready = sem("o_ready"), sem("osq_ready"), sem("g_ss_ready"), sem("g_rs_ready"), sem("og_ready")
        ogT_ready, g_mix_hi, g_mix_lo, cum_ready = sem("ogT_ready"), sem("g_mix_hi"), sem("g_mix_lo"), sem("cum_ready")
        qf_ready = sem("qf_ready")
        c_ss_ready, c_rs_ready, c_ready = sem("c_ss_ready"), sem("c_rs_ready"), sem("c_ready")
        cT_ready, cT_out, qkv_ready, qkv_out = sem("cT_ready"), sem("cT_out"), sem("qkv_ready"), sem("qkv_out")
        kpe_ready, sq_ready, h_ss_ready, h_rs_ready, qk_ready = sem("kpe_ready"), sem("sq_ready"), sem("h_ss_ready"), sem("h_rs_ready"), sem("qk_ready")
        headT_ready, qT_out, kT_out = sem("headT_ready"), sem("qT_out"), sem("kT_out")
        q_stored, k_stored, v_stored = sem("q_stored"), sem("k_stored"), sem("v_stored")
        z_stored = [sem(f"z_stored{n}") for n in range(2)]
        head_in = [sem(f"head_in{n}") for n in range(2)]
        v_in = [sem(f"v_in{n}") for n in range(2)]
        zv_in, zg_in = sem("zv_in"), sem("zg_in")
        s_ready, max_ready, p_ready, rden_ready = sem("s_ready"), sem("max_ready"), sem("p_ready"), sem("rden_ready")
        pT_ready, pT_out, pT_out2, pv_done = sem("pT_ready"), sem("pT_out"), sem("pT_out2"), sem("pv_done")
        om_ready, omT_ready = sem("om_ready"), sem("omT_ready")
        m_mix_hi, m_mix_lo = sem("m_mix_hi"), sem("m_mix_lo")
        up_ready, up_bank_free, relu_ready = sem("up_ready"), sem("up_bank_free"), sem("relu_ready")
        acthi_done, actlo_done, y_ready, y_bank_free = sem("acthi_done"), sem("actlo_done"), sem("y_ready"), sem("y_bank_free")

        block = ctx.enter_context(nc.Block())

        def raw_value(q, k):
            n = 2 * q + k // RING + 1
            return 16 * n + (16 * (k // RING + 1) if isinstance(q, int) and q == 0 else 32)

        Q_UP = IN_GROUPS + OUT_GROUPS

        OUT_ORDER = [GH + i for i in range(MH // 2 - 1)] + [0, 1, 2] + [KT - 1, 3]

        def row_tile(q, k):
            return OUT_ORDER[k] if IN_GROUPS <= q < Q_UP else k

        START = [NB - 2 + 5 * b // 2 for b in range(NB)]
        LATENTS, LATENTS_T, HEADS, HEAD_SUMS, HEAD_NORMS, HEADS_T = -1, 1, 2, 3, 4, 6

        def prep(s, stage):
            return START.index(s - stage) if s - stage in START else None

        GATE_T, LOGITS = NB + 1, NB + 3

        ORDER = [b for n in range(NB // 2) for b in (n, NB - 1 - n)]
        STEPS = [(h, b) for h in range(MH) for b in ORDER]
        SECOND = NB // 2

        def mix_due(h, n):
            if h == MH:
                return MH // 2 - 1, n
            return (h // 2 - 1, n // 2) if h % 2 == 0 and h >= 2 and n in (1, 3) else None

        def mix_part(p, half):
            last = p == MH // 2 - 1
            return GH + p, slice(half * W, (half + 1) * W), 5 if last and half else 1

        POOL_CONSTS = 4

        @block.sync
        def _(sp):
            def piece(q, k, src):
                if not (isinstance(q, int) and q == 0 and k < RING):
                    sp.wait_ge(wlo_done, KT * q + k - RING + 1)
                sp.dma_start(raw[:, k % RING, 0:src.shape[-1]], src).then_inc(raw_in[k % RING], 16)

            def in_piece(q, k):
                if q == 0:
                    piece(0, k, w_in_d[k, :, C_MLA:C_MLA + MLA_W])
                    sp.dma_start(raw[:, k % RING, MLA_W:ZM],
                                 w_in_d[k, :, C_GATE:C_GATE + GR]).then_inc(raw_in[k % RING], 16)
                else:
                    c = (C_V, C_G, C_QK)[q - 1]
                    piece(q, k, w_in_d[k, :, c:c + W])

            for k in range(KT):
                in_piece(0, k)

            def head(h):
                if h >= 2:
                    sp.wait_ge(s_ready, NB * (h - 1))
                sp.dma_start(m_qT[:, h % 2, :], q_d[h]).then_inc(head_in[h % 2], 16)
                sp.dma_start(m_kT[:, h % 2, :], k_d[h]).then_inc(head_in[h % 2], 16)

            def stores(s):
                if NB <= s < 3 * NB:
                    n = s - NB
                    sp.wait_ge(z_out, s + 1)
                    sp.dma_start(z_d[n // NB, n % NB], z_stage[:, n % 2, :]).then_inc(z_stored[n % 2], 16)
                b = prep(s, HEADS)
                if b is not None:
                    sp.wait_ge(qkv_out, b + 1)
                    sp.dma_start(v_d[b], v_stage[:, :]).then_inc(v_stored, 16)
                b = prep(s, HEADS_T)
                if b is not None:
                    blk = slice(b * P, (b + 1) * P)
                    sp.wait_ge(qT_out, b + 1)
                    sp.dma_start(q_d[:, :, blk].rearrange("h d t -> d h t"), q_stage[:, :, :]).then_inc(q_stored, 16)
                    sp.wait_ge(kT_out, b + 1)
                    sp.dma_start(k_d[:, :, blk].rearrange("h d t -> d h t"), k_stage[:, :, :]).then_inc(k_stored, 16)
                if s == START[-1] + HEADS_T:
                    sp.wait_ge(q_stored, 16 * NB)
                    sp.wait_ge(k_stored, 16 * NB)
                    sp.wait_ge(v_stored, 16 * NB)
                    head(0)
                    for n in range(2):
                        half = slice(n * NB // 2, (n + 1) * NB // 2)
                        sp.dma_start(m_v[:, half, :], v_d[half].rearrange("b p n -> p b n")).then_inc(v_in[n], 16)
                    head(1)

            for q in range(IN_GROUPS):
                if q + 1 < IN_GROUPS:
                    for k in range(RING + 2):
                        in_piece(q + 1, k)
                if q == 0:
                    sp.wait_ge(alo_done, 2 * NB)
                    sp.dma_start(m_uq[:, :, :], w_uq[0].rearrange("(k p) n -> p k n", p=P)).then_inc(mla_w_in, 16)
                    sp.dma_start(m_ukv[:, :], w_ukv[0]).then_inc(mla_w_in, 16)
                for b in range(NB - 1):
                    stores(NB * q + b)
                if q + 1 < IN_GROUPS:
                    for k in range(RING + 2, KT):
                        in_piece(q + 1, k)
                else:
                    for k in range(RING):
                        piece(IN_GROUPS, k, w_out_d[0, row_tile(IN_GROUPS, k)])
                stores(NB * q + NB - 1)

            sp.wait_ge(z_ready, NB * IN_GROUPS)
            for n in range(2):
                sp.wait_ge(z_stored[n], 16 * NB)
            sp.dma_start(zv[:, :, :], z_d[0].rearrange("b p n -> p b n")).then_inc(zv_in, 16)
            sp.dma_start(zg[:, :, :], z_d[1].rearrange("b p n -> p b n")).then_inc(zg_in, 16)
            for h in range(2, MH):
                head(h)
            for k in range(RING, KT):
                piece(IN_GROUPS, k, w_out_d[0, row_tile(IN_GROUPS, k)])
            sp.wait_ge(pv_done, len(STEPS))
            for i in range(2):
                for b in range(4 * i, 4 * i + 4):
                    sp.dma_start(xs[:, b, :], x_d[b]).then_inc(x_in[b], 16)
                for k in range(RING * i, RING * i + RING):
                    piece(IN_GROUPS + 1, k, w_out_d[1, row_tile(IN_GROUPS, k)])

            def mlp_pieces(g):
                for k in range(KT):
                    piece(Q_UP + 2 * g, k, w_up_d[g, k])
                for k in range(KT):
                    piece(Q_UP + 1 + 2 * g, k, w_down_d[g, k // NH, k % NH])

            with sp.Fori(0, FG) as g:
                mlp_pieces(g)
            for b in range(NB):
                sp.wait_ge(y_bank_free, 4 + 2 * NB * (FG - 1) + 2 * b + 2)
                sp.dma_start(out_d[b], xs[:, b, :]).then_inc(stored, 16)
            sp.wait_ge(stored, 16 * NB)

        @block.gpsimd
        def _(pool):
            steps = [0]

            def step(ins):
                steps[0] += 1
                ins.then_inc(pool_step, 1)
                pool.wait_ge(pool_step, steps[0])

            def rsqrt(dst, src, n, ready):
                step(pool.tensor_scalar(dst, src, 1.0 / n, EPS, ALU.mult, ALU.add))
                pool.tensor_tensor(dst, dst, minus_half[:, 0:dst.shape[-1]], ALU.pow).then_inc(ready, 1)

            def low_part(q, k):
                pool.wait_ge(whi_done, KT * q + k + 1)
                pool.tensor_tensor(w_lo[q % 2][:, row_tile(q, k), :], raw[:, k % RING, :], w_hi[q % 2][:, row_tile(q, k), :].bitcast(F32),
                                   ALU.subtract).then_inc(wlo_done, 1)

            def low_part_at(half, count, k):
                pool.wait_ge(whi_done, count + k + 1)
                pool.tensor_tensor(w_lo[half][:, k, :], raw[:, k % RING, :],
                                   w_hi[half][:, k, :].bitcast(F32), ALU.subtract).then_inc(wlo_done, 1)

            def in_low_part(q, k):
                width = ZM if q == 0 else W
                n = KT * q + k
                pool.wait_ge(whi_done, n + 1)
                pool.tensor_tensor(wi_lo[:, n % SLICES, 0:width], raw[:, k % RING, 0:width],
                                   wi_hi[:, n % SLICES, 0:width].bitcast(F32), ALU.subtract).then_inc(wlo_done, 1)

            pool.dma_start(gain[:, :], attn_norm[0].partition_broadcast(P)).then_inc(gain_in, 16)
            pool.dma_start(pos[:, :], positions[0].rearrange("(b p) -> p b", p=P)).then_inc(consts_in, 16)
            pool.dma_start(bg[:, :], b_gate[0].rearrange("(t p) -> p t", p=P)).then_inc(consts_in, 16)
            pool.dma_start(ga[:, 0:2], q_a_norm[0].rearrange("(t p) -> p t", p=P)).then_inc(consts_in, 16)
            pool.dma_start(ga[:, 2:3], kv_a_norm[0].rearrange("(t p) -> p t", p=P)).then_inc(consts_in, 16)
            step(pool.memset(ident[:, :], 0.0))
            pool.affine_select(out=ident[:, :], in_=ident[:, :], compare_op=ALU.not_equal, fill=1.0, base=0,
                               pattern=[[-1, P]], channel_multiplier=1).then_inc(ident_ready, 1)
            step(pool.memset(causal[:, :], 1))
            step(pool.affine_select(out=causal[:, :], in_=causal[:, :], compare_op=ALU.is_ge, fill=0.0,
                                    base=0, pattern=[[1, P]], channel_multiplier=-1))
            pool.memset(minus_half[:, :], -0.5)
            for i in range(HALF):
                last = pool.memset(freq[:, i:i + 1], float(ROPE_BASE ** (-2.0 * i / ROPE)))
            step(last)
            pool.memset(ones[:, :], 1.0).then_inc(ones_ready, 1)

            def x_rstd(b):
                pool.wait_ge(ssq_ready, b + 1)
                rsqrt(rstd[:, 0, b:b + 1], ssq[:, 0, b:b + 1], D, rstd_ready)

            x_rstd(0)
            for k in range(0, 4):
                in_low_part(0, k)
            x_rstd(1)
            for k in range(4, KT):
                in_low_part(0, k)
            for b in range(2, NB):
                x_rstd(b)
            pool.wait_ge(xn_ready, NB)
            pool.dma_start(gqk[:, 0, :], q_head_norm[0].partition_broadcast(P)).then_inc(phase_in, 16)
            pool.dma_start(gqk[:, 1, :], k_head_norm[0].partition_broadcast(P)).then_inc(phase_in, 16)
            pool.dma_start(gn[:, :], gla_out_norm[0].partition_broadcast(P)).then_inc(phase_in, 16)
            pool.dma_start(wgate[:, :], w_gate_up[0]).then_inc(phase_in, 16)
            pool.wait_ge(phase_in, 64)
            pool.tensor_scalar(gqk[:, 0, :], gqk[:, 0, :], SCALE, None, ALU.mult).then_inc(gqk_ready, 1)

            def behind(s):
                b = prep(s, LATENTS)
                if b is not None:
                    pool.wait_ge(c_ss_ready, 2 * b + 2)
                    rsqrt(c_rs[:, b, :], c_ss[:, b, :], 1.0, c_rs_ready)
                b = prep(s, LATENTS_T)
                if b is not None:
                    if b >= 2:
                        pool.wait_ge(headT_ready, 2 * (b - 1))
                    else:
                        pool.wait_ge(alo_done, 2 * NB)
                    pool.wait_ge(z_out, b + 1)
                    pool.tensor_copy(m_qk[:, b % 2, MH:2 * MH, NOPE:DQK],
                                     zm[:, b, QR + KVR:MLA_W].unsqueeze(1).broadcast_to([P, MH, ROPE])).then_inc(kpe_ready, 1)
                b = prep(s, HEAD_SUMS)
                if b is not None:
                    pool.wait_ge(h_ss_ready, b + 1)
                    rsqrt(h_rs[:, :], h_ss[:, :], 1.0, h_rs_ready)

            for q in range(IN_GROUPS):
                for b in range(NB):
                    if q + 1 < IN_GROUPS and b in (0, NB - 1):
                        for k in range(0, 2) if b == 0 else range(2, KT):
                            in_low_part(q + 1, k)
                    behind(NB * q + b)

            pool.wait_ge(z_ready, NB * IN_GROUPS)
            pool.wait_ge(kT_out, NB)
            pool.memset(sc[:, :, :], 0.0).then_inc(sc_zero, 1)
            pool.memset(state[:, :, :, :], 0.0).then_inc(sc_zero, 1)

            def decays(c):
                pool.wait_ge(qkT_out, c + 1)
                pool.wait_ge(g_exp, 4 * c + 3)
                pool.tensor_tensor(g_ke[:, c % 2, :, :], g_ke[:, c % 2, :, :], g_k[:, c % 2, :, :],
                                   ALU.mult).then_inc(ke_ready, 1)
                pool.wait_ge(g_exp, 4 * c + 4)
                pool.tensor_tensor(g_qf[:, c % 2, :, :], g_qf[:, c % 2, :, :], g_q[:, c % 2, :, :],
                                   ALU.mult).then_inc(qf_ready, 1)

            def out_rstd(c):
                pool.wait_ge(g_ss_ready, c + 1)
                rsqrt(g_rs[:, :], g_ss[:, :], GDV, g_rs_ready)

            decays(0)
            for c in range(NB):
                if c >= 1:
                    out_rstd(c - 1)
                if c + 1 < NB:
                    decays(c + 1)
            for k in range(KT - 1):
                low_part(IN_GROUPS, k)
            out_rstd(NB - 1)
            low_part(IN_GROUPS, KT - 1)
            pool.wait_ge(omT_ready, MH)
            pool.dma_start(gain[:, :], mlp_norm[0].partition_broadcast(P)).then_inc(gain_in, 16)
            for k in range(KT):
                low_part(IN_GROUPS + 1, k)
            for k in range(KT):
                low_part_at(0, KT * Q_UP, k)
            for b in range(NB):
                pool.wait_ge(ssq_ready, NB + b + 1)
                rsqrt(rstd[:, 1, b:b + 1], ssq[:, 1, b:b + 1], D, rstd_ready)
            for k in range(KT):
                low_part_at(1, KT * (Q_UP + 1), k)
            with pool.Fori(1, FG) as g:
                for half in range(2):
                    for k in range(KT):
                        low_part_at(half, KT * (Q_UP + half) + 2 * KT * g, k)

        @block.scalar
        def _(act):
            steps = [0]

            def step(ins):
                steps[0] += 1
                ins.then_inc(act_step, 1)
                act.wait_ge(act_step, steps[0])

            def copy(dst, src, scale=1.0):
                return act.activation(dst, src, ACT.Copy, scale=scale)

            def in_high_part(q, k):
                width = ZM if q == 0 else W
                n = KT * q + k
                act.wait_ge(raw_in[k % RING], raw_value(q, k))
                if n >= SLICES:
                    q0, k0 = divmod(n - SLICES, KT)
                    if k0 == KT - 1:
                        act.wait_ge(z_ready, NB * (q0 + 1))
                    else:
                        act.wait_ge(slice_free, (KT - 1) * q0 + k0 + 1)
                copy(wi_hi[:, n % SLICES, 0:width], raw[:, k % RING, 0:width]).then_inc(whi_done, 1)

            def high_part(q, k):
                act.wait_ge(raw_in[k % RING], raw_value(q, k))
                copy(w_hi[q % 2][:, row_tile(q, k), :], raw[:, k % RING, :]).then_inc(whi_done, 1)

            def high_part_at(half, g, k):
                act.wait_ge(raw_in[k % RING], 16 * (2 * (Q_UP + half) + k // RING + 1) + 32 + 64 * g)
                copy(w_hi[half][:, k, :], raw[:, k % RING, :]).then_inc(whi_done, 1)

            def square_x(r, b):
                if NB * r + b:
                    act.wait_ge(ssq_ready, NB * r + b)
                act.activation(ps[:, 6:8, :].rearrange("p a n -> p (a n)"), (xs if r else x0)[:, b, :], ACT.Square,
                               accum_out=ssq[:, r, b:b + 1]).then_inc(ssq_ready, 1)

            def norm_hi(r, b):
                for j in range(2):
                    n = 2 * (NB * r + b) + j
                    act.wait_ge(xT_ready, n + 1)
                    copy(a_hi[:, 4 * j:4 * j + 4, b * P:(b + 1) * P], bank4(4 + j)).then_inc(ahi_done, 1)

            def x_load(b):
                act.dma_start(x0[:, b, :], x_d[b]).then_inc(x_in[b], 16)

            def x_square(b):
                act.wait_ge(x_in[b], 16)
                square_x(0, b)

            def behind(s):
                if s == 1:
                    act.wait_ge(rope_arg, 1)
                    act.activation(sin[:, :, :], sin[:, :, :], ACT.Sin).then_inc(rope_ready, 1)
                    act.activation(cos[:, :, :], cos[:, :, :], ACT.Sin).then_inc(rope_ready, 1)
                b = prep(s, HEADS_T)
                if b is not None:
                    act.wait_ge(headT_ready, 2 * b + 1)
                    if b >= 1:
                        act.wait_ge(q_stored, 16 * b)
                    copy(q_stage[:, 0:4, :], bank4(4, DQK))
                    copy(q_stage[:, 4:8, :], bank4(5, DQK)).then_inc(qT_out, 1)
                b = prep(s, LATENTS)
                if b is not None:
                    act.wait_ge(z_out, b + 1)
                    for i, (c, n) in enumerate(((0, QR), (QR, KVR))):
                        if b or i:
                            act.wait_ge(c_ss_ready, 2 * b + i)
                        act.activation(junk[:, 0:n], zm[:, b, c:c + n], ACT.Square, scale=float(n) ** -0.5,
                                       accum_out=c_ss[:, b, i:i + 1]).then_inc(c_ss_ready, 1)
                b = prep(s, LATENTS_T)
                if b is not None:
                    if b == 0:
                        act.wait_ge(alo_done, 2 * NB)
                        act.wait_ge(consts_in, 64)
                    act.wait_ge(cT_ready, b + 1)
                    for i in range(3):
                        last = copy(m_cT[:, i, :], ps[:, 4, i * P:(i + 1) * P], ga[:, i:i + 1])
                    last.then_inc(cT_out, 1)
                if s == GATE_T:
                    act.wait_ge(gateT_ready, 1)
                    for i in range(2):
                        copy(zgateT[:, i * W:(i + 1) * W], ps[0:GR, 5 + i, :]).then_inc(gateT_out, 1)
                b = prep(s, HEADS)
                if b is not None:
                    qk = m_qk[:, b % 2, :, :]
                    act.wait_ge(qkv_ready, b + 1)
                    if b >= 1:
                        act.wait_ge(v_stored, 16 * b)
                    for i in range(2):
                        copy(qk[:, 4 * i:4 * i + 4, :], ps[:, 4 + i, 0:4 * DQK].rearrange("p (h d) -> p h d", d=DQK))
                    for i in range(2):
                        h = 4 * i
                        kv = bank4(6 + i)
                        copy(qk[:, MH + h:MH + h + 4, 0:NOPE], kv[:, :, 0:NOPE])
                        last = copy(v_stage[:, h * MV:(h + 4) * MV].rearrange("p (h d) -> p h d", d=MV), kv[:, :, NOPE:NOPE + MV])
                    last.then_inc(qkv_out, 1)
                    act.wait_ge(qkv_out, b + 1)
                    act.wait_ge(kpe_ready, b + 1)
                    if b >= 1:
                        act.wait_ge(h_ss_ready, b)
                    act.activation(m_sq[:, :, :], qk, ACT.Square, scale=float(DQK) ** -0.5).then_inc(sq_ready, 1)
                if s - 1 - LOGITS in range(GT):
                    t = s - 1 - LOGITS
                    act.wait_ge(logit_out, 2 * t + 2)
                    step(act.activation(g_cum[:, t, :], g_log[:, t, :], ACT.Abs))
                    step(act.activation(g_cum[:, t, :], g_cum[:, t, :], ACT.Exp, scale=-1.0))
                    act.activation(g_cum[:, t, :], g_cum[:, t, :], ACT.Ln, bias=1.0).then_inc(softplus_ready, 1)

            x_load(0)
            x_square(0)
            for k in range(2):
                in_high_part(0, k)
            x_load(1)
            for k in range(2, 4):
                in_high_part(0, k)
            norm_hi(0, 0)
            x_square(1)
            x_load(2)
            for k in range(4, KT):
                in_high_part(0, k)
            x_load(3)
            for b in range(NB):
                if b + 4 < NB:
                    x_load(b + 4)
                if b + 2 < NB:
                    x_square(b + 2)
                if b + 1 < NB:
                    norm_hi(0, b + 1)
                if b == 1:
                    for k in range(2):
                        in_high_part(1, k)
                if b == NB - 1:
                    for k in range(2, KT):
                        in_high_part(1, k)
                behind(b)
            for q in range(1, IN_GROUPS):
                for b in range(NB):
                    if q == 2:
                        act.wait_ge(z_ready, NB * q + b + 1)
                        if b >= 1:
                            act.wait_ge(z_out, NB * q + b)
                        act.activation(tanh_g[:, :], ps[:, b % 4, :], ACT.Tanh, scale=0.5).then_inc(tanh_ready, 1)
                    if q + 1 < IN_GROUPS and b in (0, NB - 1):
                        for k in range(0, 2) if b == 0 else range(2, KT):
                            in_high_part(q + 1, k)
                    behind(NB * q + b)

            def gla_exps(c):
                act.wait_ge(qkT_ready, c + 1)
                if c >= 2:
                    act.wait_ge(o_ready, c - 1)
                copy(g_q[:, c % 2, :, :], bank4(7)[:, 0:GT, :], float(GDK) ** -0.5)
                copy(g_k[:, c % 2, :, :], bank4(7)[:, GT:2 * GT, :]).then_inc(qkT_out, 1)
                cum = g_cum[:, :, c * P:(c + 1) * P]
                act.wait_ge(from_mid, c + 1)
                act.activation(g_ks[:, c % 2, :, :], g_qs[:, c % 2, :, :], ACT.Exp, scale=-1.0).then_inc(g_exp, 1)
                act.wait_ge(g_exp, 4 * c + 1)
                act.activation(g_qs[:, c % 2, :, :], g_qs[:, c % 2, :, :], ACT.Exp).then_inc(g_exp, 1)
                act.wait_ge(to_last, c + 1)
                act.activation(g_ke[:, c % 2, :, :], g_ke[:, c % 2, :, :], ACT.Exp).then_inc(g_exp, 1)
                act.activation(decay[:, :, c], cum[:, :, P - 1], ACT.Exp)
                act.activation(g_qf[:, c % 2, :, :], cum, ACT.Exp).then_inc(g_exp, 1)

            def gla_mix_hi(c):
                act.wait_ge(ogT_ready, c + 1)
                copy(a_hi[:, 0:GH, c * P:(c + 1) * P], bank4(7)).then_inc(g_mix_hi, 1)

            def gla(c, n):
                if n == 2 and c >= 1:
                    gla_mix_hi(c - 1)
                if n == 4 and c + 1 < NB:
                    act.wait_ge(keT_ready, c + 1)
                    act.wait_ge(sc_ready, 2 * c + 2)
                    copy(ke_tok[:, c, :], ps[:, 7, 2 * P:4 * P]).then_inc(keT_out, 1)
                if n == 6 and c + 1 < NB:
                    gla_exps(c + 1)
                if n == 7:
                    act.wait_ge(o_ready, c + 1)
                    if c >= 1:
                        act.wait_ge(g_ss_ready, c)
                    act.activation(osq[:, :, :], bank4(7), ACT.Square).then_inc(osq_ready, 1)

            def exp(i):
                h, b = STEPS[i]
                nk = (b + 1) * P
                act.wait_ge(max_ready, i + 1)
                if i >= 2:
                    act.wait_ge(pT_ready, 2 * (i - 1))
                act.activation(m_p[:, i % 2, 0:nk], ps[:, 2 * (i % 2):2 * (i % 2) + 2, :].rearrange("p a n -> p (a n)")[:, 0:nk],
                               ACT.Exp, bias=m_nm[:, i % 2:i % 2 + 1],
                               accum_out=m_sum[:, h % 2, b:b + 1]).then_inc(p_ready, 1)

            def mla_mix_hi(p, half):
                k, cols, bank = mix_part(p, half)
                act.wait_ge(omT_ready, 2 * p + half + 1)
                copy(a_hi[:, k, cols], ps[:, bank, :]).then_inc(m_mix_hi, 1)

            def out_high_part(k):
                if row_tile(IN_GROUPS, k) < 4:
                    act.wait_ge(og_ready, row_tile(IN_GROUPS, k) + 5)
                high_part(IN_GROUPS, k)

            act.wait_ge(cum_ready, GT)
            act.wait_ge(v_stored, 16 * NB)
            for n in range(2):
                act.wait_ge(z_stored[n], 16 * NB)
            gla_exps(0)
            exp(0)
            for i, (h, b) in enumerate(STEPS):
                turn = i % NB
                if i + 1 < len(STEPS):
                    exp(i + 1)
                act.wait_ge(pT_ready, 2 * i + 1)
                if i >= 2:
                    act.wait_ge(pv_done, i - 1)
                n = min(b + 1, 4)
                copy(m_pT[:, i % 2, 0:n, :], bank4(4)[:, 0:n, :]).then_inc(pT_out, 1)
                if mix_due(h, turn):
                    mla_mix_hi(*mix_due(h, turn))
                gla(h, turn)
                if h == MH - 1 and turn < KT - 1:
                    out_high_part(turn)
            for half in range(2):
                mla_mix_hi(*mix_due(MH, half))
            gla_mix_hi(NB - 1)
            out_high_part(KT - 1)

            for k in range(KT):
                high_part(IN_GROUPS + 1, k)
            act.wait_ge(z_ready, NB * (IN_GROUPS + 1))
            for k in range(KT):
                high_part_at(0, 0, k)
            for b in range(NB):
                act.wait_ge(z_out, NB * (Q_UP - 1) + b + 1)
                square_x(1, b)
                if b >= 1:
                    norm_hi(1, b - 1)
            norm_hi(1, NB - 1)
            act.wait_ge(z_ready, NB * Q_UP)
            act.sem_inc(up_bank_free, 4)
            for k in range(KT):
                high_part_at(1, 0, k)

            def group(g, last):
                for j in range(2 * FT):
                    f, half = j // 2, j % 2
                    act.wait_ge(up_ready, 2 * FT * g + j + 1)
                    if j >= 2:
                        act.wait_ge(actlo_done, 2 * FT * g + j - 1)
                    act.activation(relu[:, j % 2, :], ps[:, j % 4, :], ACT.Relu).then_inc(up_bank_free, 1)
                    act.wait_ge(up_bank_free, 4 + 2 * FT * g + j + 1)
                    act.activation(act_hi[:, f, half * W:(half + 1) * W], relu[:, j % 2, :],
                                   ACT.Square).then_inc(acthi_done, 1)
                if not last:
                    for k in range(KT):
                        high_part_at(0, g + 1, k)
                    act.wait_ge(y_ready, 2 * NB * g + 2 * NB)
                    for k in range(KT):
                        high_part_at(1, g + 1, k)

            with act.Fori(0, FG - 1) as g:
                group(g, False)
            group(FG - 1, True)

        @block.vector
        def _(dve):
            steps = [0]

            def step(ins):
                steps[0] += 1
                ins.then_inc(dve_step, 1)
                dve.wait_ge(dve_step, steps[0])

            def stt(out_, in0, scalar, in1, op0, op1):
                return dve.scalar_tensor_tensor(out=out_, in0=in0, scalar=scalar, in1=in1, op0=op0, op1=op1)

            def norm_x(r, b, src, dst):
                dve.wait_ge(rstd_ready, NB * r + b + 1)
                stt(dst, src[:, b, :], rstd[:, r, b:b + 1], gain[:, :], ALU.mult, ALU.mult).then_inc(xn_ready, 1)

            def norm_lo(r, b):
                for j in range(2):
                    n = 2 * (NB * r + b) + j
                    blk = slice(b * P, (b + 1) * P)
                    dve.wait_ge(ahi_done, n + 1)
                    dve.tensor_tensor(a_lo[:, 4 * j:4 * j + 4, blk], bank4(4 + j),
                                      a_hi[:, 4 * j:4 * j + 4, blk].bitcast(F32), ALU.subtract).then_inc(alo_done, 1)

            def rotary_angles():
                dve.wait_ge(consts_in, 64)
                dve.wait_ge(pool_step, POOL_CONSTS)
                step(dve.tensor_copy(rk[:, :, 0], pos[:, :]))
                for i in range(1, HALF):
                    last = dve.tensor_scalar(rk[:, :, i], rk[:, :, 0], freq[:, i:i + 1], None, ALU.mult)
                step(last)
                for table, quarter in ((sin, 0.0), (cos, 0.25)):
                    step(dve.tensor_scalar(table[:, :, :], rk[:, :, :], 1.0 / TWO_PI, quarter, ALU.mult, ALU.add))
                    step(dve.tensor_scalar(table[:, :, :], table[:, :, :], ROUND, -ROUND, ALU.add, ALU.add))
                    step(stt(rt[:, :, :], table[:, :, :], -TWO_PI_A, rk[:, :, :], ALU.mult, ALU.add))
                    step(stt(rt[:, :, :], table[:, :, :], -TWO_PI_B, rt[:, :, :], ALU.mult, ALU.add))
                    step(stt(rt[:, :, :], table[:, :, :], -TWO_PI_C, rt[:, :, :], ALU.mult, ALU.add))
                    step(dve.tensor_scalar(rt[:, :, :], rt[:, :, :], quarter * TWO_PI, PI_SAFE, ALU.add, ALU.min))
                    last = dve.tensor_scalar(table[:, :, :], rt[:, :, :], -PI_SAFE, None, ALU.max)
                    if quarter:
                        last.then_inc(rope_arg, 1)
                    else:
                        step(last)

            def tile_out(s):
                q, b = divmod(s, NB)
                dve.wait_ge(z_ready, s + 1)
                tile = ps[:, s % 4, :]
                n = s - NB
                if 2 <= n < 2 * NB:
                    dve.wait_ge(z_stored[n % 2], 16 * (n // 2))
                if q == 0:
                    dve.tensor_copy(zm[:, b, :], tile[:, 0:ZM]).then_inc(z_out, 1)
                elif q == 1:
                    dve.tensor_copy(z_stage[:, n % 2, :], tile).then_inc(z_out, 1)
                elif q == 2:
                    dve.wait_ge(phase_in, 64)
                    dve.wait_ge(tanh_ready, b + 1)
                    step(stt(z_stage[:, n % 2, :], tanh_g[:, :], 1.0, tile, ALU.add, ALU.mult))
                    g4 = z_stage[:, n % 2, :].rearrange("p (h v) -> p h v", h=GH)
                    stt(g4, g4, 0.5, gn[:, :].unsqueeze(1).broadcast_to([P, GH, GDV]), ALU.mult, ALU.mult).then_inc(z_out, 1)
                else:
                    dve.wait_ge(cum_ready, GT)
                    dve.tensor_copy(zqk[:, b, :], tile).then_inc(z_out, 1)

            def head_norms(b):
                qk = m_qk[:, b % 2, :, :]
                dve.wait_ge(h_rs_ready, b + 1)
                step(dve.tensor_tensor(qk, qk, h_rs[:, :].unsqueeze(2).broadcast_to([P, 2 * MH, DQK]), ALU.mult))
                dve.wait_ge(gqk_ready, 1)
                for i in range(2):
                    part = qk[:, i * MH:(i + 1) * MH, :]
                    last = dve.tensor_tensor(part, part, gqk[:, i, :].unsqueeze(1).broadcast_to([P, MH, DQK]), ALU.mult)
                step(last)
                dve.wait_ge(rope_ready, 2)
                pair = qk[:, :, NOPE:DQK].rearrange("p h (a i) -> p h a i", a=2)
                c = cos[:, b, :].unsqueeze(1).unsqueeze(1).broadcast_to([P, 2 * MH, 2, HALF])
                s = sin[:, b, :].unsqueeze(1).unsqueeze(1).broadcast_to([P, 2 * MH, 2, HALF])
                dve.tensor_tensor(m_rc[:, :, :, :], pair, c, ALU.mult)
                step(dve.tensor_tensor(m_rs[:, :, :, :], pair, s, ALU.mult))
                dve.tensor_tensor(pair[:, :, 0, :], m_rc[:, :, 0, :], m_rs[:, :, 1, :], ALU.subtract)
                dve.tensor_tensor(pair[:, :, 1, :], m_rs[:, :, 0, :], m_rc[:, :, 1, :], ALU.add).then_inc(qk_ready, 1)

            def gate_sums(t):
                dve.wait_ge(softplus_ready, t + 1)
                if t == 0:
                    dve.wait_ge(ones_ready, 1)
                step(stt(g_log[:, t, :], g_log[:, t, :], 0.0, g_cum[:, t, :], ALU.min, ALU.subtract))
                step(dve.tensor_scalar(g_log[:, t, :], g_log[:, t, :], 1.0 / GATE_NORM, LOG_GATE_MIN, ALU.mult, ALU.max))
                for b in range(NB):
                    blk = slice(b * P, (b + 1) * P)
                    last = dve.tensor_tensor_scan(g_cum[:, t, blk], ones[:, :], g_log[:, t, blk], 0.0, ALU.mult, ALU.add)
                last.then_inc(cum_ready, 1)

            def behind(s):
                b = prep(s, HEADS_T)
                if b is not None:
                    dve.wait_ge(headT_ready, 2 * b + 2)
                    if b >= 1:
                        dve.wait_ge(k_stored, 16 * b)
                    dve.tensor_copy(k_stage[:, 0:4, :], bank4(6, DQK))
                    dve.tensor_copy(k_stage[:, 4:8, :], bank4(7, DQK)).then_inc(kT_out, 1)
                b = prep(s, LATENTS)
                if b is not None:
                    dve.wait_ge(c_rs_ready, b + 1)
                    dve.tensor_scalar(zm[:, b, 0:QR], zm[:, b, 0:QR], c_rs[:, b, 0:1], None, ALU.mult)
                    dve.tensor_scalar(zm[:, b, QR:QR + KVR], zm[:, b, QR:QR + KVR], c_rs[:, b, 1:2], None,
                                      ALU.mult).then_inc(c_ready, 1)
                if s == LOGITS:
                    for n in range(2 * GT):
                        t, i = n // 2, n % 2
                        dve.wait_ge(logit_ready, n + 1)
                        dve.tensor_scalar(g_log[:, t, i * W:(i + 1) * W], ps[:, 4 + n, :], bg[:, t:t + 1], None,
                                          ALU.add).then_inc(logit_out, 1)
                if s - 2 - LOGITS in range(GT):
                    gate_sums(s - 2 - LOGITS)
                b = prep(s, HEAD_SUMS)
                if b is not None:
                    dve.wait_ge(sq_ready, b + 1)
                    if b >= 1:
                        dve.wait_ge(h_rs_ready, b)
                    dve.tensor_reduce(h_ss[:, :], m_sq[:, :, :], AX.X, ALU.add).then_inc(h_ss_ready, 1)
                b = prep(s, HEAD_NORMS)
                if b is not None:
                    head_norms(b)

            dve.wait_ge(gain_in, 16)
            norm_x(0, 0, x0, x0[:, 0, :])
            norm_x(0, 1, x0, x0[:, 1, :])
            norm_lo(0, 0)
            for b in range(NB):
                if b + 2 < NB:
                    norm_x(0, b + 2, x0, x0[:, b + 2, :])
                if b + 1 < NB:
                    norm_lo(0, b + 1)
                if b == 1:
                    rotary_angles()
                tile_out(b)
                behind(b)
            for s in range(NB, NB * IN_GROUPS):
                tile_out(s)
                behind(s)

            def gla_decays(c):
                cum = g_cum[:, :, c * P:(c + 1) * P]
                if c >= 2:
                    dve.wait_ge(o_ready, c - 1)
                dve.tensor_tensor(g_qs[:, c % 2, :, :], cum, cum[:, :, CHUNK - 1:CHUNK].broadcast_to([P, GT, P]),
                                  ALU.subtract).then_inc(from_mid, 1)
                dve.tensor_tensor(g_ke[:, c % 2, :, :], cum[:, :, P - 1:P].broadcast_to([P, GT, P]), cum,
                                  ALU.subtract).then_inc(to_last, 1)

            def gla_decayed(c):
                dve.wait_ge(qkT_out, c + 1)
                dve.wait_ge(g_exp, 4 * c + 2)
                dve.tensor_tensor(g_qs[:, c % 2, :, :], g_qs[:, c % 2, :, :], g_q[:, c % 2, :, :], ALU.mult).then_inc(qs_ready, 1)
                dve.tensor_tensor(g_ks[:, c % 2, :, :], g_ks[:, c % 2, :, :], g_k[:, c % 2, :, :], ALU.mult).then_inc(qs_ready, 1)

            def gla_mask(c, odd):
                dve.wait_ge(scT_ready, 2 * c + odd + 1)
                if c >= 1:
                    dve.wait_ge(o_ready, c)
                else:
                    dve.wait_ge(sc_zero, 2)
                dve.copy_predicated(sc[:, odd::2, :], causal[:, :].unsqueeze(1).broadcast_to([P, GT, P]),
                                    bank4(7)[:, 0:GT, :]).then_inc(sc_ready, 1)

            def gla_state(c):
                dve.wait_ge(kv_ready, c + 1)
                dve.wait_ge(g_exp, 4 * c + 4)
                if c >= 1:
                    dve.wait_ge(o_ready, c)
                    dve.wait_ge(state_ready, c)
                for t in range(GT):
                    for s in range(2):
                        rows = slice(s * GDK, (s + 1) * GDK)
                        kv = ps[rows, 7, (2 * t + s) * GDV:(2 * t + s + 1) * GDV]
                        own = slice(s * GDV, (s + 1) * GDV)
                        last = stt(state[rows, (c + 1) % 2, t, own], state[rows, c % 2, t, own],
                                   decay[rows, t, c:c + 1], kv, ALU.mult, ALU.add)
                last.then_inc(state_ready, 1)

            def gla_sums(c):
                dve.wait_ge(osq_ready, c + 1)
                if c >= 1:
                    dve.wait_ge(g_rs_ready, c)
                dve.tensor_reduce(g_ss[:, :], osq[:, :, :], AX.X, ALU.add).then_inc(g_ss_ready, 1)

            def gla_out(c):
                dve.wait_ge(g_rs_ready, c + 1)
                if c >= 1:
                    dve.wait_ge(ogT_ready, c)
                else:
                    dve.wait_ge(zg_in, 16)
                step(dve.tensor_tensor(og[:, :, :], bank4(7), g_rs[:, :].unsqueeze(2).broadcast_to([P, GH, GDV]), ALU.mult))
                g4 = zg[:, c, :].rearrange("p (h v) -> p h v", h=GH)
                dve.tensor_tensor(og[:, :, :], og[:, :, :], g4, ALU.mult).then_inc(og_ready, 1)

            def gla_lo(c):
                blk = slice(c * P, (c + 1) * P)
                dve.wait_ge(g_mix_hi, c + 1)
                dve.tensor_tensor(a_lo[:, 0:GH, blk], bank4(7), a_hi[:, 0:GH, blk].bitcast(F32),
                                  ALU.subtract).then_inc(g_mix_lo, 1)

            def gla(c, n):
                if c >= 1 and n <= 2:
                    (gla_sums, gla_out, gla_lo)[n](c - 1)
                if n in (3, 4):
                    gla_mask(c, n - 3)
                if c + 1 < NB:
                    if n == 5:
                        gla_state(c)
                    if n == 6:
                        gla_decays(c + 1)
                    if n == 7:
                        gla_decayed(c + 1)

            def row_max(i):
                h, b = STEPS[i]
                nk = (b + 1) * P
                s = ps[:, 2 * (i % 2):2 * (i % 2) + 2, :].rearrange("p a n -> p (a n)")
                dve.wait_ge(s_ready, i + 1)
                step(dve.memset(s[0:CHUNK, nk - CHUNK:nk], MASKED))
                if i >= 2:
                    dve.wait_ge(p_ready, i - 1)
                dve.tensor_reduce(m_nm[:, i % 2:i % 2 + 1], s[:, 0:nk], AX.X, ALU.max, negate=True).then_inc(max_ready, 1)

            def head_out(h):
                dve.wait_ge(p_ready, NB * (h + 1))
                if h >= 1:
                    dve.wait_ge(om_ready, h)
                dve.reciprocal(m_rden[:, :], m_sum[:, h % 2, :]).then_inc(rden_ready, 1)
                dve.wait_ge(rden_ready, h + 1)
                dve.wait_ge(pv_done, NB * (h + 1))
                if h >= 2:
                    dve.wait_ge(omT_ready, 2 * (h // 2))
                dve.tensor_tensor(om[:, :, (h % 2) * MV:(h % 2 + 1) * MV], ps[:, 6, :].rearrange("p (b v) -> p b v", b=NB),
                                  m_rden[:, :].unsqueeze(2).broadcast_to([P, NB, MV]), ALU.mult).then_inc(om_ready, 1)

            def mla_mix_lo(p, half):
                k, cols, bank = mix_part(p, half)
                dve.wait_ge(m_mix_hi, 2 * p + half + 1)
                dve.tensor_tensor(a_lo[:, k, cols], ps[:, bank, :], a_hi[:, k, cols].bitcast(F32),
                                  ALU.subtract).then_inc(m_mix_lo, 1)

            dve.wait_ge(z_stored[1], 16 * NB)
            gla_decays(0)
            gla_decayed(0)
            row_max(0)
            row_max(1)
            for i, (h, b) in enumerate(STEPS):
                turn = i % NB
                if i + 2 < len(STEPS):
                    row_max(i + 2)
                if b >= SECOND:
                    dve.wait_ge(pT_ready, 2 * i + 2)
                    if i >= 2:
                        dve.wait_ge(pv_done, i - 1)
                    dve.tensor_copy(m_pT[:, i % 2, 4:b + 1, :], bank4(5)[:, 0:b - 3, :]).then_inc(pT_out2, 1)
                if turn == 0 and h >= 1:
                    head_out(h - 1)
                if mix_due(h, turn):
                    mla_mix_lo(*mix_due(h, turn))
                gla(h, turn)
            gla_sums(NB - 1)
            head_out(MH - 1)
            mla_mix_lo(*mix_due(MH, 0))
            gla_out(NB - 1)
            mla_mix_lo(*mix_due(MH, 1))
            gla_lo(NB - 1)

            def residual(n, b):
                m = NB * (IN_GROUPS + n) + b
                dve.wait_ge(z_ready, m + 1)
                if n == 0:
                    dve.wait_ge(x_in[b], 32)
                xh = xs[:, b, n * W:(n + 1) * W]
                dve.tensor_tensor(xh, ps[:, m % 4, :], xh, ALU.add).then_inc(z_out, 1)

            for b in range(NB):
                residual(0, b)
            dve.wait_ge(gain_in, 32)
            for b in range(NB):
                residual(1, b)
                if b >= 1:
                    if b - 1 >= 2:
                        dve.wait_ge(xT_ready, 2 * (NB + b - 2))
                    norm_x(1, b - 1, xs, xn2[:, (b - 1) % 2, :])
                if b >= 2:
                    norm_lo(1, b - 2)
            dve.wait_ge(xT_ready, 2 * (NB + NB - 2))
            norm_x(1, NB - 1, xs, xn2[:, (NB - 1) % 2, :])
            norm_lo(1, NB - 2)
            norm_lo(1, NB - 1)
            dve.sem_inc(y_bank_free, 4)

            def group(g):
                for j in range(2 * FT):
                    f, half = j // 2, j % 2
                    cols = slice(half * W, (half + 1) * W)
                    dve.wait_ge(acthi_done, 2 * FT * g + j + 1)
                    dve.tensor_tensor(relu[:, j % 2, :], relu[:, j % 2, :], relu[:, j % 2, :],
                                      ALU.mult).then_inc(relu_ready, 1)
                    dve.wait_ge(relu_ready, 2 * FT * g + j + 1)
                    dve.tensor_tensor(act_lo[:, f, cols], relu[:, j % 2, :], act_hi[:, f, cols].bitcast(F32),
                                      ALU.subtract).then_inc(actlo_done, 1)
                for t in range(2 * NB):
                    b, n = t // 2, t % 2
                    dve.wait_ge(y_ready, 2 * NB * g + t + 1)
                    xh = xs[:, b, n * W:(n + 1) * W]
                    dve.tensor_tensor(xh, ps[:, 4 + t % 4, :], xh, ALU.add).then_inc(y_bank_free, 1)

            with dve.Fori(0, FG) as g:
                group(g)

        @block.tensor
        def _(pe):
            def mm(dst, lhsT, rhs, start, stop):
                return pe.matmul(dst, lhsT, rhs, start=start, stop=stop)

            def split_product(dst, hi, lo, rhs_hi, rhs_lo, first, last):
                mm(dst, hi, rhs_hi, first, False)
                mm(dst, hi, rhs_lo, False, False)
                return mm(dst, lo, rhs_hi, False, last)

            def norm_T(r, b, src):
                pe.wait_ge(xn_ready, NB * r + b + 1)
                for j in range(2):
                    n = 2 * (NB * r + b) + j
                    if n >= 2:
                        pe.wait_ge(alo_done, n - 1)
                    for i in range(4):
                        last = pe.transpose(bank4(4 + j)[:, i, :], src[:, (4 * j + i) * P:(4 * j + i + 1) * P], ident[:, :])
                    last.then_inc(xT_ready, 1)

            def in_project(q, b):
                n = NB * q + b
                blk = slice(b * P, (b + 1) * P)
                width = ZM if q == 0 else W
                if n >= 4:
                    pe.wait_ge(z_out, n - 3)
                for k in range(KT):
                    if b == 0:
                        pe.wait_ge(wlo_done, KT * q + k + 1)
                    w = (KT * q + k) % SLICES
                    last = split_product(ps[:, n % 4, 0:width], a_hi[:, k, blk], a_lo[:, k, blk],
                                         wi_hi[:, w, 0:width], wi_lo[:, w, 0:width], k == 0, k == KT - 1)
                    if b == NB - 1 and k < KT - 1:
                        last.then_inc(slice_free, 1)
                last.then_inc(z_ready, 1)

            def project(q, b, between=None):
                n = NB * q + b
                blk = slice(b * P, (b + 1) * P)
                pe.wait_ge(z_out, n - 3)
                if q == IN_GROUPS and b == 1:
                    pe.wait_ge(m_mix_lo, MH - 1)
                for k in range(KT):
                    if between is not None and k == 3:
                        between()
                    tile = row_tile(q, k)
                    if q == IN_GROUPS and tile == 0:
                        pe.wait_ge(g_mix_lo, b + 1)
                    if q == IN_GROUPS and tile == KT - 1:
                        pe.wait_ge(m_mix_lo, MH - 1 if b < NB // 2 else MH)
                    if b == 0:
                        pe.wait_ge(wlo_done, KT * q + k + 1)
                    last = split_product(ps[:, n % 4, :], a_hi[:, tile, blk], a_lo[:, tile, blk],
                                         w_hi[q % 2][:, tile, :], w_lo[q % 2][:, tile, :], k == 0, k == KT - 1)
                last.then_inc(z_ready, 1)

            def behind(s):
                b = prep(s, HEADS_T)
                if b is not None:
                    pe.wait_ge(qk_ready, b + 1)
                    pe.wait_ge(qkv_out, min(b + 2, NB))
                    if b == 0:
                        pe.wait_ge(logit_out, 4)
                    if b == NB - 1:
                        pe.wait_ge(qT_out, b)
                        pe.wait_ge(kT_out, b)
                    for i in range(2 * MH):
                        last = pe.transpose(bank4(4 + i // 4, DQK)[:, i % 4, :], m_qk[:, b % 2, i, :], ident[:, :])
                        if i % MH == MH - 1:
                            last.then_inc(headT_ready, 1)
                b = prep(s, LATENTS_T)
                if b is not None:
                    pe.wait_ge(c_ready, b + 1)
                    if b == 0:
                        pe.wait_ge(alo_done, 2 * NB)
                    else:
                        pe.wait_ge(qkv_out, b)
                    if b >= 2:
                        pe.wait_ge(qT_out, b - 1)
                    for i in range(3):
                        last = pe.transpose(ps[:, 4, i * P:(i + 1) * P], zm[:, b, i * P:(i + 1) * P], ident[:, :])
                    last.then_inc(cT_ready, 1)
                b = prep(s, HEADS)
                if b is not None:
                    if b == 0:
                        pe.wait_ge(mla_w_in, 32)
                        pe.wait_ge(ssq_ready, NB)
                    elif b == 1:
                        pe.wait_ge(gateT_out, 2)
                    else:
                        pe.wait_ge(kT_out, b - 1)
                    pe.wait_ge(cT_out, b + 1)
                    for j in range(2):
                        for i in range(QR // P):
                            mm(ps[:, 4 + j, 0:4 * DQK], m_cT[:, i, :], m_uq[:, i, 4 * j * DQK:4 * (j + 1) * DQK],
                               i == 0, i == QR // P - 1)
                    for j in range(2):
                        last = mm(ps[:, 6 + j, :], m_cT[:, 2, :], m_ukv[:, j * W:(j + 1) * W], True, True)
                    last.then_inc(qkv_ready, 1)
                if s == GATE_T:
                    pe.wait_ge(z_out, NB)
                    pe.wait_ge(qkv_out, 1)
                    for b in range(NB):
                        last = pe.transpose(bank4(5 + b // 4, GR)[:, b % 4, :], zm[:, b, MLA_W:ZM], ident[:, :])
                    last.then_inc(gateT_ready, 1)
                if s == LOGITS:
                    pe.wait_ge(qkv_out, 2)
                    pe.wait_ge(phase_in, 64)
                    for n in range(2 * GT):
                        t, i = n // 2, n % 2
                        mm(ps[:, 4 + n, :], wgate[:, t * P:(t + 1) * P], zgateT[:, i * W:(i + 1) * W],
                           True, True).then_inc(logit_ready, 1)

            pe.wait_ge(ident_ready, 1)
            norm_T(0, 0, x0[:, 0, :])
            for b in range(NB):
                if b + 1 < NB:
                    norm_T(0, b + 1, x0[:, b + 1, :])
                pe.wait_ge(alo_done, 2 * b + 2)
                in_project(0, b)
                behind(b)
            for q in range(1, IN_GROUPS):
                for b in range(NB):
                    in_project(q, b)
                    behind(NB * q + b)

            def gla_qkT(c):
                if c >= 1:
                    pe.wait_ge(state_ready, c)
                for i in range(2 * GT):
                    last = pe.transpose(bank4(7)[:, i, :], zqk[:, c, i * P:(i + 1) * P], ident[:, :])
                last.then_inc(qkT_ready, 1)

            def gla_scores(c, odd):
                rows = slice(odd * GDK, (odd + 1) * GDK)
                for t in range(GT):
                    last = mm(bank4(7)[:, t, :], g_ks[rows, c % 2, t, :], g_qs[rows, c % 2, t, :], True, True)
                last.then_inc(scT_ready, 1)

            def gla(c, n):
                if n == 2 and c >= 1:
                    pe.wait_ge(og_ready, c)
                    for h in range(GH):
                        last = pe.transpose(bank4(7)[:, h, :], og[:, h, :], ident[:, :])
                    last.then_inc(ogT_ready, 1)
                if n == 3:
                    pe.wait_ge(qs_ready, 2 * c + 2)
                    if c >= 1:
                        pe.wait_ge(g_mix_lo, c)
                    gla_scores(c, 0)
                if n == 4:
                    pe.wait_ge(sc_ready, 2 * c + 1)
                    if c + 1 < NB:
                        pe.wait_ge(ke_ready, c + 1)
                        for t in range(GT):
                            last = pe.transpose(bank4(7)[:, GT + t, :], g_ke[:, c % 2, t, :], ident[:, :])
                        last.then_inc(keT_ready, 1)
                    gla_scores(c, 1)
                if n == 5 and c + 1 < NB:
                    pe.wait_ge(keT_out, c + 1)
                    if c == 0:
                        pe.wait_ge(zv_in, 16)
                    for t in range(GT):
                        last = mm(ps[:, 7, 2 * t * GDV:2 * (t + 1) * GDV], ke_tok[:, c, t * P:(t + 1) * P],
                                  zv[:, c, 2 * t * GDV:2 * (t + 1) * GDV], True, True)
                    last.then_inc(kv_ready, 1)
                if n == 6 and c + 1 < NB:
                    gla_qkT(c + 1)
                if n == 7:
                    pe.wait_ge(qf_ready, c + 1)
                    if c + 1 < NB:
                        pe.wait_ge(qkT_out, c + 2)
                    else:
                        pe.wait_ge(sc_ready, 2 * NB)
                    for t in range(GT):
                        mm(ps[:, 7, 2 * t * GDV:2 * (t + 1) * GDV], g_qf[:, c % 2, t, :], state[:, c % 2, t, :],
                           True, False)
                        for h in (2 * t, 2 * t + 1):
                            last = mm(bank4(7)[:, h, :], sc[:, h, :], zv[:, c, h * GDV:(h + 1) * GDV],
                                      False, h % 2 == 1)
                    last.then_inc(o_ready, 1)

            def scores(i):
                h, b = STEPS[i]
                nk = (b + 1) * P
                if i >= 2:
                    pe.wait_ge(p_ready, i - 1)
                if i % NB == 0:
                    pe.wait_ge(head_in[h % 2], 32 * (h // 2 + 1))
                for c in range(0, nk, W):
                    n = min(W, nk - c)
                    last = mm(ps[:, 2 * (i % 2) + c // W, 0:n], m_qT[:, h % 2, b * P:(b + 1) * P],
                              m_kT[:, h % 2, c:c + n], True, True)
                last.then_inc(s_ready, 1)

            def p_transposes(i):
                h, b = STEPS[i]
                pe.wait_ge(p_ready, i + 1)
                if i >= 1:
                    pe.wait_ge(pT_out, i)
                if b >= SECOND and i // 2:
                    pe.wait_ge(pT_out2, i // 2)
                for c in range(b + 1):
                    last = pe.transpose(bank4(4 + c // 4)[:, c % 4, :], m_p[:, i % 2, c * P:(c + 1) * P], ident[:, :])
                    if c == min(b, 3):
                        last.then_inc(pT_ready, 1 if b >= SECOND else 2)
                if b >= SECOND:
                    last.then_inc(pT_ready, 1)

            def values(i):
                h, b = STEPS[i]
                pe.wait_ge(pT_out, i + 1)
                if b >= SECOND:
                    pe.wait_ge(pT_out2, i // 2 + 1)
                if i == 0:
                    pe.wait_ge(v_in[0], 16)
                if i == 1:
                    pe.wait_ge(v_in[1], 16)
                if i % NB == 0 and h >= 1:
                    pe.wait_ge(om_ready, h)
                for c in range(b + 1):
                    last = mm(ps[:, 6, b * MV:(b + 1) * MV], m_pT[:, i % 2, c, :], m_v[:, c, h * MV:(h + 1) * MV],
                              c == 0, c == b)
                last.then_inc(pv_done, 1)

            def mix_T(p, half):
                pe.wait_ge(om_ready, 2 * p + 2)
                _, _, bank = mix_part(p, half)
                if bank == 5:
                    pe.wait_ge(pT_out2, len(STEPS) // 2)
                elif p or half:
                    pe.wait_ge(m_mix_lo, 2 * p + half)
                for j in range(4):
                    last = pe.transpose(bank4(bank)[:, j, :], om[:, 4 * half + j, :], ident[:, :])
                last.then_inc(omT_ready, 1)

            pe.wait_ge(z_out, NB * IN_GROUPS)
            pe.wait_ge(qT_out, NB)
            pe.wait_ge(kT_out, NB)
            gla_qkT(0)
            scores(0)
            scores(1)
            for i, (h, b) in enumerate(STEPS):
                turn = i % NB
                if i + 2 < len(STEPS):
                    scores(i + 2)
                p_transposes(i)
                if i >= 1:
                    values(i - 1)
                if mix_due(h, turn):
                    mix_T(*mix_due(h, turn))
                gla(h, turn)
            values(len(STEPS) - 1)

            def last_mixes():
                for half in range(2):
                    mix_T(*mix_due(MH, half))
                gla(NB, 2)

            for n in range(NH):
                for b in range(NB):
                    project(IN_GROUPS + n, b, last_mixes if n == b == 0 else None)
                    if n == NH - 1 and b >= 2:
                        norm_T(1, b - 2, xn2[:, b % 2, :])
            norm_T(1, NB - 2, xn2[:, NB % 2, :])
            norm_T(1, NB - 1, xn2[:, (NB - 1) % 2, :])

            def group(g, first):
                for j in range(2 * FT):
                    f, half = j // 2, j % 2
                    cols = slice(half * W, (half + 1) * W)
                    pe.wait_ge(up_bank_free, 2 * FT * g + j + 1)
                    for k in range(KT):
                        if j == 0:
                            pe.wait_ge(wlo_done, 2 * KT * g + KT * Q_UP + k + 1)
                        wh = w_hi[0][:, k, f * P:(f + 1) * P]
                        wl = w_lo[0][:, k, f * P:(f + 1) * P]
                        last = split_product(ps[:, j % 4, :], wh, wl, a_hi[:, k, cols], a_lo[:, k, cols],
                                             k == 0, k == KT - 1)
                    last.then_inc(up_ready, 1)
                for quad in range(NB // 2):
                    for f in range(FT):
                        pe.wait_ge(actlo_done, 2 * FT * g + 2 * f + quad // 2 + 1)
                        for s in range(4):
                            t = 4 * quad + s
                            b, n = t // 2, t % 2
                            blk = slice(b * P, (b + 1) * P)
                            if f == 0:
                                pe.wait_ge(y_bank_free, 2 * NB * g + t + 1)
                            if quad == 0 and s < 2:
                                pe.wait_ge(wlo_done, 2 * KT * g + KT * (Q_UP + 1) + 2 * f + n + 1)
                            kk = 2 * f + n
                            last = split_product(ps[:, 4 + s, :], act_hi[:, f, blk], act_lo[:, f, blk],
                                                 w_hi[1][:, kk, :], w_lo[1][:, kk, :], f == 0, f == FT - 1)
                            if f == FT - 1:
                                last.then_inc(y_ready, 1)

            pe.wait_ge(alo_done, 4 * NB)
            with pe.Fori(0, FG) as g:
                group(g, False)


_INS = ['x', 'positions', 'attn_norm', 'w_in', 'w_gate_up', 'b_gate', 'gla_out_norm', 'q_a_norm', 'w_uq',
        'kv_a_norm', 'w_ukv', 'q_head_norm', 'k_head_norm', 'w_out', 'mlp_norm', 'w_up', 'w_down']


def kernel(**inputs):
    import numpy as _np
    import concourse.bacc as _bacc
    from concourse import mybir as _mybir
    from concourse.bass_utils import run_bass_kernel_spmd as _run

    nc = _bacc.Bacc("TRN2", target_bir_lowering=False, num_devices=1)
    arrays, args = {}, []
    for name in _INS:
        a = _np.ascontiguousarray(inputs[name])
        arrays[f"in_{name}_dram"] = a
        args.append(nc.dram_tensor(f"in_{name}_dram", a.shape, _mybir.dt.from_np(a.dtype), kind="ExternalInput").ap())
    out = nc.dram_tensor("out_0_dram", (1, T, D), F32, kind="ExternalOutput").ap()
    layer(nc, *args, out)
    r = _run(nc, [arrays], core_ids=[0])
    return r.results[0]["out_0_dram"]
```
